# Optimizing a Trainium2 kernel written in Bass

```python
import jax, jax.numpy as jnp
from jax import lax
import numpy as np

D_MODEL = 1024
BATCH = 1
SEQ = 512
DEPTH = 2

CHUNK = 64
CONV_W = 4
BR_W = 512
N_BRANCH = 3
DN_HEADS = 4
DN_DK = 128
DN_DV = 128
LRU_W = BR_W
LRU_BLOCKS = 8
LRU_BLK = LRU_W // LRU_BLOCKS
LRU_C = 8.0
LA_HEADS = 8
LA_HD = 64
LA_PAST = 8
LA_BAND = (LA_PAST + 1) * CHUNK
REL_CLIP = 128
MEM_LEN = 256
XA_HEADS = 4
XA_HD = D_MODEL // XA_HEADS
D_FF = 2816
ALPHA = (2 * DEPTH) ** 0.25
BETA = (8 * DEPTH) ** -0.25
LN_EPS = 1e-5
NORM_EPS = 1e-6
NEG_INF = -1e30

SPLITS = (DN_HEADS * DN_DK, DN_HEADS * DN_DK, DN_HEADS * DN_DV, DN_HEADS * DN_DV,
          DN_HEADS, DN_HEADS, LRU_W, LRU_W, LA_HEADS * LA_HD, LA_HEADS * LA_HD,
          LA_HEADS * LA_HD, N_BRANCH * D_MODEL)
N_IN = sum(SPLITS)

kernel_name = "hybrid_deltanet_rglru_chunkattn_deepnorm"

def layer_norm(x, g, b):
    xf = x.astype(jnp.float32)
    mu = xf.mean(-1, keepdims=True)
    var = jnp.square(xf - mu).mean(-1, keepdims=True)
    return ((xf - mu) * lax.rsqrt(var + LN_EPS) * g.astype(jnp.float32)
            + b.astype(jnp.float32)).astype(x.dtype)

def swiglu(x, w12, w3):
    g, u = jnp.split(x @ w12, 2, axis=-1)
    return (jax.nn.silu(g) * u) @ w3

def causal_dwconv(x, w):
    c = x.shape[-1]
    return lax.conv_general_dilated(
        x, w[:, None, :].astype(x.dtype), window_strides=(1,),
        padding=[(CONV_W - 1, 0)], dimension_numbers=('NWC', 'WIO', 'NWC'),
        feature_group_count=c)

def l2norm(t):
    return t * lax.rsqrt(jnp.sum(t * t, axis=-1, keepdims=True) + NORM_EPS)

def chunk_gated_delta(q, k, v, g, beta):
    b_, s_, h, dk = q.shape
    dv = v.shape[-1]
    n = s_ // CHUNK

    def chunks(t):
        t = t.reshape((b_, n, CHUNK, h) + t.shape[3:])
        return jnp.moveaxis(t, (1, 3), (0, 2))

    qc, kc, vc = chunks(q), chunks(k), chunks(v)
    G = jnp.cumsum(chunks(g), axis=-1)
    bc = chunks(beta)
    idx = jnp.arange(CHUNK)
    causal = idx[:, None] >= idx[None, :]
    decay = jnp.exp(jnp.where(causal, G[..., :, None] - G[..., None, :], -jnp.inf))
    kb = kc * bc[..., None]
    m = jnp.einsum('nbhid,nbhjd->nbhij', kb, kc) * decay
    m = jnp.where(idx[:, None] > idx[None, :], m, 0.0) + jnp.eye(CHUNK, dtype=m.dtype)
    rhs = jnp.concatenate([vc * bc[..., None], kb * jnp.exp(G)[..., None]], axis=-1)
    sol = lax.linalg.triangular_solve(m, rhs, left_side=True, lower=True,
                                      unit_diagonal=True)
    u, w = sol[..., :dv], sol[..., dv:]
    qk = jnp.einsum('nbhid,nbhjd->nbhij', qc, kc) * decay
    q_dec = qc * jnp.exp(G)[..., None]
    k_dec = kc * jnp.exp(G[..., -1:] - G)[..., None]
    g_last = jnp.exp(G[..., -1])

    def step(state, inp):
        qd, kd, u_i, w_i, qk_i, gl = inp
        v_new = u_i - jnp.einsum('bhck,bhkv->bhcv', w_i, state)
        o = (jnp.einsum('bhck,bhkv->bhcv', qd, state)
             + jnp.einsum('bhij,bhjv->bhiv', qk_i, v_new))
        state = state * gl[..., None, None] + jnp.einsum('bhck,bhcv->bhkv', kd, v_new)
        return state, o

    state0 = jnp.zeros((b_, h, dk, dv), jnp.float32)
    _, o = lax.scan(step, state0, (q_dec, k_dec, u, w, qk, g_last))
    return jnp.moveaxis(o, (0, 2), (1, 3)).reshape(b_, s_, h, dv)

def gated_deltanet(q, k, v, z, b, a, conv_w, a_log, dt_bias, norm_w):
    f32 = jnp.float32
    b_, s_ = q.shape[:2]
    qkv = jax.nn.silu(causal_dwconv(jnp.concatenate([q, k, v], axis=-1), conv_w))
    q, k, v = jnp.split(qkv.astype(f32), [DN_HEADS * DN_DK, 2 * DN_HEADS * DN_DK], axis=-1)
    q = l2norm(q.reshape(b_, s_, DN_HEADS, DN_DK)) * (DN_DK ** -0.5)
    k = l2norm(k.reshape(b_, s_, DN_HEADS, DN_DK))
    v = v.reshape(b_, s_, DN_HEADS, DN_DV)
    beta = jax.nn.sigmoid(b.astype(f32))
    g = -jnp.exp(a_log.astype(f32)) * jax.nn.softplus(a.astype(f32) + dt_bias.astype(f32))
    o = chunk_gated_delta(q, k, v, g, beta)
    zf = z.reshape(b_, s_, DN_HEADS, DN_DV).astype(f32)
    o = (o * lax.rsqrt(jnp.mean(o * o, axis=-1, keepdims=True) + NORM_EPS)
         * norm_w.astype(f32) * jax.nn.silu(zf))
    return o.reshape(b_, s_, DN_HEADS * DN_DV).astype(z.dtype)

def _lin_combine(e1, e2):
    a1, b1 = e1
    a2, b2 = e2
    return a1 * a2, a2 * b1 + b2

def rglru_branch(xb, gate_in, conv_w, conv_b, gate_w, gate_b, lam):
    f32 = jnp.float32
    b_, s_ = xb.shape[:2]
    xc = (causal_dwconv(xb, conv_w) + conv_b).astype(f32)
    blk = xc.reshape(b_, s_, LRU_BLOCKS, LRU_BLK)
    gates = jnp.einsum('bsnd,gnde->gbsne', blk, gate_w.astype(f32))
    gates = gates.reshape(2, b_, s_, LRU_W) + gate_b.astype(f32)[:, None, None, :]
    r = jax.nn.sigmoid(gates[0])
    i = jax.nn.sigmoid(gates[1])
    log_a = -LRU_C * r * jax.nn.softplus(-lam.astype(f32))
    a = jnp.exp(log_a)
    u = xc * i * jnp.sqrt(-jnp.expm1(2.0 * log_a))
    _, h = lax.associative_scan(_lin_combine, (a, u), axis=1)
    return (h * jax.nn.gelu(gate_in.astype(f32))).astype(xb.dtype)

def chunk_band_attention(q, k, v, rel_table):
    b_, s_ = q.shape[:2]
    n = s_ // CHUNK
    shp = (b_, n, CHUNK, LA_HEADS, LA_HD)
    q, k, v = q.reshape(shp), k.reshape(shp), v.reshape(shp)
    pad = ((0, 0), (LA_PAST, 0), (0, 0), (0, 0), (0, 0))
    kp, vp = jnp.pad(k, pad), jnp.pad(v, pad)
    kb = jnp.concatenate([kp[:, w:w + n] for w in range(LA_PAST + 1)], axis=2)
    vb = jnp.concatenate([vp[:, w:w + n] for w in range(LA_PAST + 1)], axis=2)
    s = jnp.einsum('bnqhd,bnkhd->bhnqk', q, kb,
                   preferred_element_type=jnp.float32) * (LA_HD ** -0.5)
    qi = jnp.arange(CHUNK)[:, None]
    kj = jnp.arange(LA_BAND)[None, :]
    rel = kj - LA_PAST * CHUNK - qi
    bias = rel_table.astype(jnp.float32)[:, jnp.clip(rel, -REL_CLIP, REL_CLIP) + REL_CLIP]
    valid = (jnp.arange(n)[:, None] - LA_PAST + kj // CHUNK) >= 0
    s = jnp.where(valid[None, None, :, None, :], s + bias[None, :, None], NEG_INF)
    p = jax.nn.softmax(s, axis=-1).astype(v.dtype)
    o = jnp.einsum('bhnqk,bnkhd->bnqhd', p, vb)
    return o.reshape(b_, s_, LA_HEADS * LA_HD)

def hybrid_mixer(x, w_in, dn_conv_w, dn_a_log, dn_dt_bias, dn_norm_w, lru_conv_w,
                 lru_conv_b, lru_gate_w, lru_gate_b, lru_lambda, la_rel_bias,
                 w_branch, w_out):
    b_, s_ = x.shape[:2]
    proj = x @ w_in
    (dq, dk, dv, dz, db, da, lx, lg, aq, ak, av, gl) = jnp.split(
        proj, np.cumsum(SPLITS)[:-1].tolist(), axis=-1)
    ya = gated_deltanet(dq, dk, dv, dz, db, da, dn_conv_w, dn_a_log, dn_dt_bias, dn_norm_w)
    yb = rglru_branch(lx, lg, lru_conv_w, lru_conv_b, lru_gate_w, lru_gate_b, lru_lambda)
    yc = chunk_band_attention(aq, ak, av, la_rel_bias)
    up = jnp.einsum('bsrc,rcd->bsrd', jnp.stack([ya, yb, yc], axis=2), w_branch)
    gates = jax.nn.sigmoid(gl.astype(jnp.float32)).reshape(b_, s_, N_BRANCH, D_MODEL)
    merged = jnp.sum(gates.astype(x.dtype) * up, axis=2)
    return merged @ w_out

def memory_cross_attention(x, mem, wq, wkv, wo):
    b_, s_ = x.shape[:2]
    q = (x @ wq).reshape(b_, s_, XA_HEADS, XA_HD)
    k, v = jnp.split(mem @ wkv, 2, axis=-1)
    k = k.reshape(b_, MEM_LEN, XA_HEADS, XA_HD)
    v = v.reshape(b_, MEM_LEN, XA_HEADS, XA_HD)
    s = jnp.einsum('bshd,bmhd->bhsm', q, k,
                   preferred_element_type=jnp.float32) * (XA_HD ** -0.5)
    p = jax.nn.softmax(s, axis=-1).astype(v.dtype)
    o = jnp.einsum('bhsm,bmhd->bshd', p, v).reshape(b_, s_, D_MODEL)
    return o @ wo

def setup_inputs(seed: int = 0) -> dict:
    key = jax.random.key(seed)
    ks = jax.random.split(key, 24)
    f32 = jnp.float32

    def nrm(k, shape, fan_in, scale=1.0):
        return jax.random.normal(k, shape, f32) * (scale * fan_in ** -0.5)

    x = jax.random.normal(ks[0], (BATCH, SEQ, D_MODEL), f32)
    mem = jax.random.normal(ks[1], (BATCH, MEM_LEN, D_MODEL), f32)
    ln_g = 1.0 + 0.02 * jax.random.normal(ks[2], (DEPTH, 4, D_MODEL), f32)
    ln_b = 0.02 * jax.random.normal(ks[3], (DEPTH, 4, D_MODEL), f32)
    ffn_w12 = nrm(ks[4], (DEPTH, 2, D_MODEL, 2 * D_FF), D_MODEL)
    ffn_w3 = nrm(ks[5], (DEPTH, 2, D_FF, D_MODEL), D_FF, BETA)
    mix_w_in = nrm(ks[6], (DEPTH, D_MODEL, N_IN), D_MODEL)
    dn_conv_w = nrm(ks[7], (DEPTH, CONV_W, 2 * DN_HEADS * DN_DK + DN_HEADS * DN_DV), CONV_W)
    dn_a_log = jnp.log(jax.random.uniform(ks[8], (DEPTH, DN_HEADS), f32, 1.0, 16.0))
    dt = jnp.exp(jax.random.uniform(ks[9], (DEPTH, DN_HEADS), f32,
                                    float(np.log(1e-3)), float(np.log(1e-1))))
    dn_dt_bias = dt + jnp.log(-jnp.expm1(-dt))
    dn_norm_w = 1.0 + 0.02 * jax.random.normal(ks[10], (DEPTH, DN_DV), f32)
    lru_conv_w = nrm(ks[11], (DEPTH, CONV_W, LRU_W), CONV_W)
    lru_conv_b = 0.01 * jax.random.normal(ks[12], (DEPTH, LRU_W), f32)
    lru_gate_w = nrm(ks[13], (DEPTH, 2, LRU_BLOCKS, LRU_BLK, LRU_BLK), LRU_BLK)
    lru_gate_b = 0.01 * jax.random.normal(ks[14], (DEPTH, 2, LRU_W), f32)
    a_c = jax.random.uniform(ks[15], (DEPTH, LRU_W), f32, 0.9, 0.999)
    a0 = a_c ** (1.0 / LRU_C)
    lru_lambda = jnp.log(a0) - jnp.log1p(-a0)
    la_rel_bias = 0.1 * jax.random.normal(ks[16], (DEPTH, LA_HEADS, 2 * REL_CLIP + 1), f32)
    w_branch = nrm(ks[17], (DEPTH, N_BRANCH, BR_W, D_MODEL), BR_W)
    mix_w_out = nrm(ks[18], (DEPTH, D_MODEL, D_MODEL), D_MODEL, BETA)
    xa_wq = nrm(ks[19], (DEPTH, D_MODEL, D_MODEL), D_MODEL)
    xa_wkv = nrm(ks[20], (DEPTH, D_MODEL, 2 * D_MODEL), D_MODEL)
    xa_wo = nrm(ks[21], (DEPTH, D_MODEL, D_MODEL), D_MODEL, BETA)
    return {"x": x, "mem": mem, "ln_g": ln_g, "ln_b": ln_b, "ffn_w12": ffn_w12,
            "ffn_w3": ffn_w3, "mix_w_in": mix_w_in, "dn_conv_w": dn_conv_w,
            "dn_a_log": dn_a_log, "dn_dt_bias": dn_dt_bias, "dn_norm_w": dn_norm_w,
            "lru_conv_w": lru_conv_w, "lru_conv_b": lru_conv_b, "lru_gate_w": lru_gate_w,
            "lru_gate_b": lru_gate_b, "lru_lambda": lru_lambda, "la_rel_bias": la_rel_bias,
            "w_branch": w_branch, "mix_w_out": mix_w_out, "xa_wq": xa_wq,
            "xa_wkv": xa_wkv, "xa_wo": xa_wo}

def reference(x, mem, ln_g, ln_b, ffn_w12, ffn_w3, mix_w_in, dn_conv_w, dn_a_log,
              dn_dt_bias, dn_norm_w, lru_conv_w, lru_conv_b, lru_gate_w, lru_gate_b,
              lru_lambda, la_rel_bias, w_branch, mix_w_out, xa_wq, xa_wkv, xa_wo):
    for l in range(DEPTH):
        x = layer_norm(ALPHA * x + 0.5 * swiglu(x, ffn_w12[l, 0], ffn_w3[l, 0]),
                       ln_g[l, 0], ln_b[l, 0])
        y = hybrid_mixer(x, mix_w_in[l], dn_conv_w[l], dn_a_log[l], dn_dt_bias[l],
                         dn_norm_w[l], lru_conv_w[l], lru_conv_b[l], lru_gate_w[l],
                         lru_gate_b[l], lru_lambda[l], la_rel_bias[l], w_branch[l],
                         mix_w_out[l])
        x = layer_norm(ALPHA * x + y, ln_g[l, 1], ln_b[l, 1])
        x = layer_norm(ALPHA * x + memory_cross_attention(x, mem, xa_wq[l], xa_wkv[l], xa_wo[l]),
                       ln_g[l, 2], ln_b[l, 2])
        x = layer_norm(ALPHA * x + 0.5 * swiglu(x, ffn_w12[l, 1], ffn_w3[l, 1]),
                       ln_g[l, 3], ln_b[l, 3])
    return x


_drawn_inputs = setup_inputs


def setup_inputs(seed=0):
    import zlib

    import numpy as np

    out = dict(_drawn_inputs(seed))
    spreads = {}
    factors = {'dn_norm_w': 8.0, 'lru_conv_b': 7.068, 'lru_gate_b': 64.0, 'la_rel_bias': 8.0}
    for name, (base, spread) in spreads.items():
        noise = np.random.default_rng([zlib.crc32(name.encode()), seed]).standard_normal(out[name].shape)
        drawn = base * np.exp(spread * noise) if base else spread * noise
        out[name] = __import__('jax').numpy.asarray(drawn.astype(out[name].dtype))
    for name, factor in factors.items():
        out[name] = (out[name] * factor).astype(out[name].dtype)
    return out
```

```python
from contextlib import ExitStack, contextmanager

import numpy as np

import concourse.bass as bass
from concourse import mybir

F32 = mybir.dt.float32
F32R = mybir.dt.float32r
ALU = mybir.AluOpType
ACT = mybir.ActivationFunctionType
AX = mybir.AxisListType

P = 128
DEPTH = 2
SEQ = 512
DM = 1024
KD = DM // P
FF = 2816
KF = FF // P
BRW = 512
KB = BRW // P
NBR = 3
HA = 8
HDA = 64
HX = 4
MEM = 256
KM = MEM // P
HN = 4
CH = SEQ // P
REL = 128
ALPHA = (2 * DEPTH) ** 0.25
LN_EPS = 1e-5
NORM_EPS = 1e-6
NEG = -1e30
LRU_C = 8.0
DELTA_LINKS, MERGE_LINKS, LAYER_LINKS = 9, 4, 219

UNIT = 1024
SLOTS = 4
LEVELS = 7

PHASES = [("ffn_up0", 2 * KF, 2 * KF), ("ffn_down0", KD, 3 * KD), ("att_qk", 2 * KB, 2 * KB),
          ("att_v", CH, CH), ("lru_x", KB, KB), ("lru_g", KB, KB), ("delta", 4 * HN, 4 * HN),
          ("merge", 6 * KD, 5 * KD), ("mix_out", KD, KD), ("mem_k", KD, KD), ("mem_v", 4, KD),
          ("x_q", KD, KD), ("x_out", KD, KD), ("ffn_up1", 2 * KF, 2 * KF), ("ffn_down1", KD, 3 * KD)]
TILE0, UNIT0 = {}, {}
_t = _u = 0
for _name, _tiles, _units in PHASES:
    TILE0[_name], UNIT0[_name] = _t, _u
    _t, _u = _t + _tiles, _u + _units
TILES, UNITS = _t, _u

OWNER = {"ffn_up0": "d", "ffn_down0": "d", "att_qk": "a", "att_v": "a", "lru_x": "a", "lru_g": "a", "delta": "a",
         "merge": "both", "mix_out": "d", "mem_k": "a", "mem_v": "a", "x_q": "a", "x_out": "d",
         "ffn_up1": "d", "ffn_down1": "d"}
FREE_D, FREE_A = {}, {}
_d = _a = 0
for _name, _tiles, _units in PHASES:
    FREE_D[_name], FREE_A[_name] = _d, _a
    _d += {"d": _tiles, "a": 0, "both": _tiles // 2}[OWNER[_name]]
    _a += {"a": _tiles, "d": 0, "both": _tiles // 2}[OWNER[_name]]
FREED_D, FREED_A = _d, _a

P_LNG, P_LNB = 0, 4 * KD
P_CW = P_LNB + 4 * KD
P_LCW = P_CW + HN * 12
P_LCB = P_LCW + KB * 4
P_GB = P_LCB + KB
P_LAM = P_GB + 2 * KB
P_NW = P_LAM + KB
P_ALOG = P_NW + 1
P_DT = P_ALOG + 1
PAR = P_DT + 1

C_ID, C_CAUSAL, C_FLIP, C_LEVEL = 0, P, 2 * P, 3 * P
CONST = (3 + LEVELS) * P


class Signal:

    def __init__(self, handle, per_layer, start=0):
        self.sem, self.per_layer, self.start = handle, per_layer, start

    def at(self, layer, n):
        return layer * self.per_layer + (self.start + n)


class StepSignal:

    def __init__(self, handle, steps, rounds):
        self.sem, self.steps, self.rounds, self.next = handle, steps, rounds, 0

    def after(self, layer, rnd, step):
        n = len(self.steps)
        return layer * (n * self.rounds) + rnd * n + (self.steps.index(step) + 1)

    def done(self, ins, step):
        assert self.steps[self.next % len(self.steps)] == step, (step, self.steps[self.next % len(self.steps)])
        self.next += 1
        return ins.then_inc(self.sem, 1)


class Chain:

    def __init__(self, eng, handle):
        self.eng, self.sem, self.base, self.n = eng, handle, 0, 0

    def link(self, ins):
        self.n += 1
        ins.then_inc(self.sem, 1)
        self.eng.wait_ge(self.sem, self.base + self.n)

    @contextmanager
    def loop(self, count, links):
        with self.eng.Fori(0, count) as i:
            base, n = self.base, self.n
            self.base = base + i * links
            yield i
            assert self.n - n == links, f"{self.n - n} links in the loop's body, not {links}"
            self.base, self.n = base, n + count * links


DN_PE = (["norm_sums", "decay_rows", "norm_q", "norm_k", "k_turned", "v_turned", "a01", "a23", "inv0_turned"]
         + [f"{x}{s}" for s in range(1, LEVELS) for x in (("p", "qt", "q") if s < LEVELS - 1 else ("p", "qt"))]
         + ["w"] + [f"{x}{c}" for c in range(CH) for x in (("v", "o", "s") if c < CH - 1 else ("v", "o"))]
         + ["rms_sums", "rms_rows"])
DN_ACT = (["th0", "th1", "th2", "sq_q", "sq_k", "norm_std", "exp_g", "decay_exp", "kd_exp", "last_exp", "kg", "vk",
           "inv0"] + [f"p{s}" for s in range(1, LEVELS)] + ["w", "o", "o_sq", "rms_std", "z_th", "y_hi"])
DN_DVE = (["conv0", "conv1", "conv2", "silu0", "silu1", "silu2", "g_row", "norm_rec", "q_normed", "k_normed",
           "g_last", "decay_min", "kd_arg", "q_dec", "decay", "kd", "m", "qk", "c0", "t0"]
          + [f"{x}{s}" for s in range(1, LEVELS) for x in (("c", "t", "n") if s < LEVELS - 1 else ("c", "t"))]
          + [f"{x}{c}" for c in range(CH) for x in (("v", "s") if c < CH - 1 else ("v",))]
          + ["rms_rec", "o_normed", "z_gate", "y", "y_lo"])
LRU_ACT = ([f"{x}{p}" for p in range(KB) for x in ("r", "i", "a", "s")]
           + [f"q{p}" for p in range(KB)] + [f"{x}{p}" for p in range(KB) for x in ("g_sq", "g_th", "y_hi")])
LRU_DVE = ([f"conv{p}" for p in range(KB)] + [f"{x}{p}" for p in range(KB) for x in ("q", "xi")]
           + [f"h{p}" for p in range(KB)] + [f"{x}{p}" for p in range(KB) for x in ("g_arg", "y", "y_lo")])



def trunk(nc, xT, memT, stream, par_d, ba_w_d, gate_w_d, table_d, const_d, ext_d, outT):
    with ExitStack() as ctx:
        def sem(name):
            return ctx.enter_context(nc.semaphore(name))

        def sb(name, shape, dt=F32, scope=ctx):
            return scope.enter_context(nc.sbuf_tensor(name, shape, dt))

        xf = sb("xf", [P, KD, SEQ])
        xh = sb("xh", [P, KD, SEQ], F32R)
        xl = sb("xl", [P, KD, SEQ], F32R)
        raw = sb("raw", [P, SLOTS, UNIT])
        wh = sb("wh", [P, SLOTS, UNIT], F32R)
        wl = sb("wl", [P, SLOTS, UNIT], F32R)
        const = sb("const", [P, CONST])
        par = sb("par", [P, PAR])
        tmp = [sb(f"tmp{n}", [P, SEQ]) for n in range(4)]
        sq_hi = sb("sq_hi", [P, SEQ], F32R)
        sq_lo = sb("sq_lo", [P, SEQ], F32R)
        ones = sb("ones", [P, P])
        mean_w = sb("mean_w", [P, P], F32R)
        zero_w = sb("zero_w", [P, P], F32R)
        row_of = sb("row_of", [P, 2, 32])
        eps_rms = sb("eps_rms", [P, 1])
        eps_l2 = sb("eps_l2", [P, 1])
        eps_0 = sb("eps_0", [P, 1])
        warm = sb("warm", [P, 1])

        with ExitStack() as ffn:
            hh = sb("hh", [P, KF, SEQ], F32R, ffn)
            hl = sb("hl", [P, KF, SEQ], F32R, ffn)
        with ExitStack() as mix:
            ych = sb("ych", [P, 2 * KB, SEQ], F32R, mix)
            ycl = sb("ycl", [P, 2 * KB, SEQ], F32R, mix)
            with ExitStack() as att:
                aq = sb("aq", [P, KB, SEQ], F32, att)
                ak = sb("ak", [P, KB, SEQ], F32, att)
                av = sb("av", [P, CH, BRW], F32, att)
                bias = sb("bias", [P, HA, 2 * P], F32, att)
                ext = sb("ext", [HA, 3 * P - 1], F32, att)
                sc = sb("sc", [P, CH, SEQ], F32, att)
                pt = sb("pt", [P, CH, SEQ], F32, att)
                neg_max = sb("neg_max", [P, HA * CH], F32, att)
                row_sum = sb("row_sum", [P, HA * CH], F32, att)
                inv_sum = sb("inv_sum", [P, HA * CH], F32, att)
            with ExitStack() as lru:
                lx = sb("lx", [P, KB, SEQ + 3], F32, lru)
                lc = sb("lc", [P, KB, SEQ], F32, lru)
                lr = sb("lr", [P, KB, SEQ], F32, lru)
                li = sb("li", [P, KB, SEQ], F32, lru)
                la = sb("la", [P, KB, SEQ], F32, lru)
                lg = sb("lg", [P, KB, SEQ], F32, lru)
                gate_w = sb("gate_w", [P, 2, KB, P], F32, lru)
                lam = sb("lam", [P, 8, KB], F32, lru)
            yah = sb("yah", [P, KB, SEQ], F32R, mix)
            yal = sb("yal", [P, KB, SEQ], F32R, mix)
            with ExitStack() as dn:
                dx = sb("dx", [P, 3, SEQ + 3], F32, dn)
                dc = sb("dc", [P, 3, SEQ], F32, dn)
                dz = sb("dz", [P, SEQ], F32, dn)
                rows = sb("rows", [P, SEQ], F32, dn)
                grow = sb("grow", [32, SEQ], F32, dn)
                eg = sb("eg", [P, SEQ], F32, dn)
                dt_ = sb("decay", [P, CH, P], F32, dn)
                mt = sb("mt", [P, CH, P], F32, dn)
                qk = sb("qk", [P, CH, P], F32, dn)
                tt = sb("tt", [P, CH, P], F32, dn)
                kg = sb("kg", [P, CH, P], F32, dn)
                kd = sb("kd", [P, CH, P], F32, dn)
                vk = sb("vk", [P, CH, P], F32, dn)
                qd = sb("qd", [P, SEQ], F32, dn)
                os_ = sb("os", [P, SEQ], F32, dn)
                state = sb("state", [P, P], F32, dn)
                vn = sb("vn", [P, P], F32, dn)
                ba_w = sb("ba_w", [P, KD, 64], F32, dn)
                cols = sb("cols", [P, 3, CH, HN], F32, dn)
                hc = sb("hc", [P, 2, CH], F32, dn)
                nea = sb("nea", [32, 2], F32, dn)
            with ExitStack() as mrg:
                gt = sb("gt", [P, 2, NBR, SEQ], F32, mrg)
                mh = sb("mh", [P, KD, SEQ], F32R, mrg)
                ml = sb("ml", [P, KD, SEQ], F32R, mrg)
        with ExitStack() as xa:
            xq = sb("xq", [P, KD, SEQ], F32, xa)
            oh = sb("oh", [P, KD, SEQ], F32R, xa)
            ol = sb("ol", [P, KD, SEQ], F32R, xa)
            mraw = sb("mraw", [P, KD, MEM], F32, xa)
            meh = sb("meh", [P, KD, MEM], F32R, xa)
            mel = sb("mel", [P, KD, MEM], F32R, xa)
            xk = sb("xk", [P, KD, MEM], F32, xa)
            x_negmax = sb("x_negmax", [P, HX * CH], F32, xa)
            x_sum = sb("x_sum", [P, HX * CH], F32, xa)
            x_inv = sb("x_inv", [P, HX * CH], F32, xa)
        xv = mraw[:, :, :].rearrange("p k m -> p (k m)").rearrange("p (a f) -> p a f", a=KM)

        ident = const[:, C_ID:C_ID + P]
        flip = const[:, C_FLIP:C_FLIP + P]
        causal = const[:, C_CAUSAL:C_CAUSAL + P]

        def level_mask(s):
            m = const[:, C_LEVEL + s * P:C_LEVEL + (s + 1) * P]
            return m.rearrange("p (a b) -> p a b", a=1).broadcast_to([P, CH, P])

        x_loaded, const_loaded, par_loaded = sem("x_loaded"), sem("const_loaded"), sem("par_loaded")
        mix_par_loaded = [sem(f"mix_par_loaded{n}") for n in range(3)]
        ext_stored, bias_loaded, mem_loaded, out_stored = sem("ext_stored"), sem("bias_loaded"), sem("mem_loaded"), sem("out_stored")
        unit_loaded = [sem(f"unit_loaded{s}") for s in range(SLOTS)]
        hi_step, unit_split, unit_begun = sem("hi_step"), sem("unit_split"), sem("unit_begun")
        consts_set, waited_apart = sem("consts_set"), sem("waited_apart")
        acc_ready = Signal(sem("acc_ready"), TILES)
        freed_d = Signal(sem("freed_d"), FREED_D, start=4)
        freed_a = Signal(sem("freed_a"), FREED_A, start=4)
        silu_th = Signal(sem("silu_th"), 2 * KF)
        inner_hi = Signal(sem("inner_hi"), 2 * KF)
        inner_lo = Signal(sem("inner_lo"), 2 * KF)
        y_hi, y_sq, y_sq_hi = (Signal(sem(n), 4 * KD) for n in ("y_hi", "y_sq", "y_sq_hi"))
        y_lo, y_sq_lo, stat_added = (Signal(sem(n), 4 * KD) for n in ("y_lo", "y_sq_lo", "stat_added"))
        variance, deviation = Signal(sem("variance"), 4), Signal(sem("deviation"), 4)
        centred, affine = Signal(sem("centred"), 4 * KD), Signal(sem("affine"), 4 * KD)
        x_hi, x_lo = Signal(sem("x_hi"), 4 * KD, KD), Signal(sem("x_lo"), 4 * KD, KD)
        ext_padded = Signal(sem("ext_padded"), 1)
        bias_flipped, bias_copied = Signal(sem("bias_flipped"), 4), Signal(sem("bias_copied"), 4)
        bias_masked = Signal(sem("bias_masked"), 1)
        scores = Signal(sem("scores"), HA * CH)
        biased, row_max = Signal(sem("biased"), HA * CH), Signal(sem("row_max"), HA * CH)
        exps, probs = Signal(sem("exps"), HA * CH), Signal(sem("probs"), HA * CH)
        turned, turned_out = Signal(sem("turned"), HA * CH), Signal(sem("turned_out"), HA * CH)
        att_out = Signal(sem("att_out"), HA)
        yc_hi, yc_lo = Signal(sem("yc_hi"), KB), Signal(sem("yc_lo"), KB)
        lru_act, lru_dve = StepSignal(sem("lru_act"), LRU_ACT, 1), StepSignal(sem("lru_dve"), LRU_DVE, 1)
        lru_gates = Signal(sem("lru_gates"), 2 * KB)
        lam_arg, lam_exp, lam_ready = (Signal(sem(n), 1) for n in ("lam_arg", "lam_exp", "lam_ready"))
        ba_ready, rows_turned = Signal(sem("ba_ready"), 1), Signal(sem("rows_turned"), 1)
        row_arg, row_exp, rows_ready, cols_ready = (Signal(sem(n), 1) for n in ("row_arg", "row_exp", "rows_ready", "cols_ready"))
        beta_th, cols_exp = Signal(sem("beta_th"), 1), Signal(sem("cols_exp"), 1)
        dn_pe, dn_act, dn_dve = (StepSignal(sem(n), steps, HN) for n, steps in (("dn_pe", DN_PE), ("dn_act", DN_ACT), ("dn_dve", DN_DVE)))
        merged, merged_hi, merged_lo = (Signal(sem(n), KD) for n in ("merged", "merged_hi", "merged_lo"))
        mem_hi, mem_lo = Signal(sem("mem_hi"), 1), Signal(sem("mem_lo"), 1)
        x_scores, x_row_max, x_exps, x_probs, x_turned, x_turned_out = (
            Signal(sem(n), HX * CH) for n in ("x_scores", "x_row_max", "x_exps", "x_probs", "x_turned", "x_turned_out"))
        x_att_out, xo_hi, xo_lo = (Signal(sem(n), 2 * HX) for n in ("x_att_out", "xo_hi", "xo_lo"))
        dve_step, act_step = sem("dve_step"), sem("act_step")

        acc = ctx.enter_context(nc.psum_tensor("acc", [P, 4, SEQ], F32))
        aux = ctx.enter_context(nc.psum_tensor("aux", [P, 4, SEQ], F32))
        B4, B5, B6, B7 = (aux[:, n, :] for n in range(4))

        def x_sc(n):
            return tmp[(n % 4) // 2][:, (n % 2) * MEM:(n % 2 + 1) * MEM]

        def tiles(bank):
            bank = bank[:, :]
            return bank.rearrange("p (c m) -> p c m", c=CH)

        def wait_apart(eng, sem_, value):
            eng.wait_ge(sem_, value)
            eng.sem_inc(waited_apart, 1)

        ROUNDS = DEPTH * UNITS // SLOTS
        block = ctx.enter_context(nc.Block())

        @block.sync
        def _(sp):
            sp.dma_start(xf[:, :, :], xT.rearrange("(k p) t -> p k t", p=P)).then_inc(x_loaded, 16)
            for s in range(SLOTS):
                sp.dma_start(raw[:, s, :], stream[s]).then_inc(unit_loaded[s], 16)
            with sp.Fori(1, ROUNDS) as i:
                for s in range(SLOTS):
                    sp.wait_ge(unit_split, i * SLOTS + (s - SLOTS + 1))
                    sp.dma_start(raw[:, s, :], stream[i * SLOTS + s]).then_inc(unit_loaded[s], 16)
            sp.wait_ge(x_hi.sem, x_hi.start + DEPTH * x_hi.per_layer)
            sp.dma_start(outT.rearrange("(k p) t -> p k t", p=P), xf[:, :, :]).then_inc(out_stored, 16)
            sp.wait_ge(out_stored, 16)

        @block.gpsimd
        def _(pool):
            pool.dma_start(const[:, :], const_d).then_inc(const_loaded, 16)
            pool.memset(ones[:, :], 1.0).then_inc(consts_set, 1)
            pool.memset(mean_w[:, :].bitcast(F32), 1.0 / DM).then_inc(consts_set, 1)
            pool.memset(zero_w[:, :].bitcast(F32), 0.0).then_inc(consts_set, 1)
            pool.memset(row_of[:, :, :], 0.0).then_inc(consts_set, 1)
            pool.memset(eps_rms[:, :], NORM_EPS).then_inc(consts_set, 1)
            pool.memset(eps_l2[:, :], 4 * NORM_EPS).then_inc(consts_set, 1)
            pool.memset(eps_0[:, :], 0.0).then_inc(consts_set, 1)
            pool.wait_ge(consts_set, 7)
            for r in range(2):
                pool.memset(row_of[:, r, r:r + 1], 1.0).then_inc(consts_set, 1)

            def split(i, s):
                pool.tensor_scalar(wh[:, s, :], raw[:, s, :], 1.0, 0.0, ALU.mult, ALU.add).then_inc(hi_step, 1)
                pool.wait_ge(hi_step, i * SLOTS + (s + 1))
                pool.tensor_tensor(wl[:, s, :], raw[:, s, :], wh[:, s, :].bitcast(F32), ALU.subtract).then_inc(unit_split, 1)

            for s in range(SLOTS):
                pool.wait_ge(unit_loaded[s], 16)
                split(0, s)
            with pool.Fori(1, ROUNDS) as i:
                for s in range(SLOTS):
                    pool.wait_ge(unit_loaded[s], i * 16 + 16)
                    wait_apart(pool, unit_begun, i * SLOTS + (s - SLOTS + 2))
                    split(i, s)

        @block.tensor
        def _(pe):
            def mm(out, w, x, start=True, stop=True):
                return pe.matmul(out, w, x, start=start, stop=stop, skip_group_check=True)

            def three(out, w_hi, w_lo, x_hi_, x_lo_, start, stop, begins=False):
                first = mm(out, w_hi, x_hi_, start, False)
                if begins:
                    first.then_inc(unit_begun, 1)
                mm(out, w_hi, x_lo_, False, False)
                return mm(out, w_lo, x_hi_, False, stop)

            def unit_here(layer, u):
                pe.wait_ge(unit_split, layer * UNITS + (u + 1))

            def unit(out, s, k_tiles, at, rhs, start, stop, ready=None, begins=True):
                for n, k in enumerate(k_tiles):
                    if ready is not None:
                        ready(k)
                    c = slice((at + n) * P, (at + n + 1) * P)
                    last = three(out, wh[:, s, c], wl[:, s, c], *rhs(k), start and n == 0,
                                 stop and n == len(k_tiles) - 1, begins=begins and n == 0)
                return last

            def of_x(k):
                return xh[:, k, :], xl[:, k, :]

            def x_ready(l, norm):
                return lambda k: pe.wait_ge(x_lo.sem, x_lo.at(l, (norm - 1) * KD + k + 1))

            def free_bank(l, name, t):
                sig, base = (freed_d, FREE_D[name]) if OWNER[name] == "d" else (freed_a, FREE_A[name])
                pe.wait_ge(sig.sem, sig.at(l, base) + t)

            def simple_tile(l, name, n, ready=None, cols=slice(0, SEQ), rhs=of_x, i=0):
                free_bank(l, name, i * 4 + (n - 3))
                unit_here(l, i * 4 + (UNIT0[name] + n))
                unit(acc[:, n % 4, cols], n % SLOTS, range(KD), 0, rhs, True, True, ready).then_inc(acc_ready.sem, 1)

            def clear_statistics(l, norm):
                zeros = zero_w[:, :].rearrange("p (a b) -> p a b", a=1).broadcast_to([P, 4, P])
                mm(B4, zero_w[:, :], zeros, True, False)
                mm(B5, zero_w[:, :], zeros, True, False)

            def add_statistics(l, norm, i, n):
                d = i * 4 + n
                pe.wait_ge(y_lo.sem, y_lo.at(l, norm * KD + 1) + d)
                mm(B4, mean_w[:, :], xh[:, d, :], False, False)
                mm(B4, mean_w[:, :], xl[:, d, :], False, False)
                pe.wait_ge(y_sq_lo.sem, y_sq_lo.at(l, norm * KD + 1) + d)
                mm(B5, mean_w[:, :], sq_hi[:, :], False, False)
                mm(B5, mean_w[:, :], sq_lo[:, :], False, False).then_inc(stat_added.sem, 1)

            def out_projection(l, name, norm, tile):
                clear_statistics(l, norm)
                with pe.Fori(0, KD // 4) as i:
                    for n in range(4):
                        free_bank(l, name, i * 4 + (n - 3))
                        tile(i, n).then_inc(acc_ready.sem, 1)
                        if n >= 1:
                            add_statistics(l, norm, i, n - 1)
                    add_statistics(l, norm, i, 3)

            def one_unit(l, name, rhs, ready):
                def tile(i, n):
                    unit_here(l, i * 4 + (UNIT0[name] + n))
                    return unit(acc[:, n, :], n, range(KD), 0, rhs, True, True, ready if n == 0 else None)
                return tile

            def ffn(l, which, norm):
                up, down = f"ffn_up{which}", f"ffn_down{which}"
                with pe.Fori(0, KF // 2) as i:
                    for n in range(4):
                        simple_tile(l, up, n, x_ready(l, norm) if n == 0 else None, i=i)

                def inner_ready(k):
                    pe.wait_ge(inner_lo.sem, inner_lo.at(l, which * KF + k + 1))

                def tile(i, n):
                    parts = [range(0, 8), range(8, 16), range(16, KF)]
                    for m, ks in enumerate(parts):
                        unit_here(l, i * 12 + (UNIT0[down] + 3 * n + m))
                        last = unit(acc[:, n, :], (3 * n + m) % SLOTS, ks, 0, lambda k: (hh[:, k, :], hl[:, k, :]),
                                    m == 0, m == 2, inner_ready if n == 0 else None)
                    return last
                out_projection(l, down, norm, tile)

            def attention(l):
                for n in range(2 * KB):
                    simple_tile(l, "att_qk", n, x_ready(l, 1) if n == 0 else None)
                for t in range(CH):
                    free_bank(l, "att_v", t - 3)
                for n in range(4):
                    unit_here(l, UNIT0["att_v"] + n)
                    for t in range(CH):
                        for m in range(2):
                            k, c = 2 * n + m, slice(m * BRW, (m + 1) * BRW)
                            tok = slice(t * P, (t + 1) * P)
                            o = acc[:, t, :]
                            first = mm(o, xh[:, k, tok], wh[:, n, c], k == 0, False)
                            if t == 0 and m == 0:
                                first.then_inc(unit_begun, 1)
                            mm(o, xh[:, k, tok], wl[:, n, c], False, False)
                            last = mm(o, xl[:, k, tok], wh[:, n, c], False, k == KD - 1)
                        if n == 3:
                            last.then_inc(acc_ready.sem, 1)

                pe.wait_ge(freed_a.sem, freed_a.at(l, FREE_A["att_v"] + CH))

                pe.wait_ge(bias_loaded, l * 16 + 16)
                for m in range(4):
                    mm(aux[:, m, :], flip, bias[:, 2 * m:2 * m + 2, :]).then_inc(bias_flipped.sem, 1)
                pe.wait_ge(bias_copied.sem, bias_copied.at(l, 4))

                def score(n):
                    h, i = divmod(n, CH)
                    rows_ = slice(HDA * (h % 2), HDA * (h % 2) + HDA)
                    if n >= 2:
                        pe.wait_ge(biased.sem, biased.at(l, n - 1))
                    mm(aux[:, n % 2, 0:(i + 1) * P], aq[rows_, h // 2, i * P:(i + 1) * P],
                       ak[rows_, h // 2, 0:(i + 1) * P]).then_inc(scores.sem, 1)

                def turn(n):
                    h, i = divmod(n, CH)
                    pe.wait_ge(probs.sem, probs.at(l, n + 1))
                    if n >= 2:
                        pe.wait_ge(turned_out.sem, turned_out.at(l, n - 1))
                    for j in range(i + 1):
                        last = pe.transpose(aux[:, 2 + n % 2, j * P:(j + 1) * P], sc[:, i, j * P:(j + 1) * P], ident)
                    last.then_inc(turned.sem, 1)

                def values(h):
                    bank = acc[HDA * (h % 2):HDA * (h % 2) + HDA, (h // 2) % 2, :]
                    pe.wait_ge(turned_out.sem, turned_out.at(l, CH * (h + 1)))
                    if h % 2 == 0 and h >= 4:
                        pe.wait_ge(yc_lo.sem, yc_lo.at(l, h // 2 - 1))
                    for j in range(CH):
                        last = mm(bank[:, j * P:SEQ], av[:, j, h * HDA:(h + 1) * HDA], pt[:, j, j * P:SEQ],
                                  j == 0, j == CH - 1)
                    last.then_inc(att_out.sem, 1)

                score(0)
                score(1)
                for n in range(HA * CH):
                    turn(n)
                    if n + 2 < HA * CH:
                        score(n + 2)
                    if n % CH == CH - 1:
                        values(n // CH)
                pe.wait_ge(yc_lo.sem, yc_lo.at(l, KB))

            def rg_lru(l):
                for n in range(KB):
                    simple_tile(l, "lru_x", n)
                for n in range(KB):
                    simple_tile(l, "lru_g", n)
                for p in range(KB):
                    pe.wait_ge(lru_dve.sem, lru_dve.after(l, 0, f"conv{p}"))
                    if p == 0:
                        pe.wait_ge(mix_par_loaded[0], l * 16 + 16)
                    if p >= 2:
                        pe.wait_ge(lru_act.sem, lru_act.after(l, 0, f"i{p - 2}"))
                    for g in range(2):
                        mm(aux[:, 2 * (p % 2) + g, :], gate_w[:, g, p, :], lc[:, p, :]).then_inc(lru_gates.sem, 1)

            def delta_rows(l):
                pe.wait_ge(mix_par_loaded[1], l * 16 + 16)
                pe.wait_ge(lru_act.sem, lru_act.after(l, 0, "i3"))
                for k in range(KD):
                    last = mm(B7[0:64, :], ba_w[:, k, :], xf[:, k, :], k == 0, k == KD - 1)
                last.then_inc(ba_ready.sem, 1)
                pe.wait_ge(rows_ready.sem, rows_ready.at(l, 1))
                for c in range(CH):
                    last = pe.transpose(tiles(B6)[:, c, :], rows[:, c * P:(c + 1) * P], ident)
                last.then_inc(rows_turned.sem, 1)

            def delta(l):
                with pe.Fori(0, HN) as h:
                    def dve(step):
                        pe.wait_ge(dn_dve.sem, dn_dve.after(l, h, step))

                    def act(step):
                        pe.wait_ge(dn_act.sem, dn_act.after(l, h, step))

                    done = dn_pe.done

                    for n in range(4):
                        simple_tile(l, "delta", n, i=h)
                    act("sq_q")
                    mm(B4[0:32, :], row_of[:, 0, :], tmp[0][:, :], True, False)
                    act("sq_k")
                    done(mm(B4[0:32, :], row_of[:, 1, :], tmp[1][:, :], False, True), "norm_sums")
                    dve("g_row")
                    done(mm(B5, ones[0:HN, :], grow[0:HN, :]), "decay_rows")
                    dve("norm_rec")
                    for r, bank in enumerate((B6, B7)):
                        done(mm(bank, ident[0:2, r:r + 1].broadcast_to([2, P]), tmp[3][0:2, :]), ("norm_q", "norm_k")[r])
                    dve("k_normed")
                    act("norm_std")
                    for c in range(CH):
                        last = pe.transpose(tiles(B4)[:, c, :], dc[:, 1, c * P:(c + 1) * P], ident)
                    done(last, "k_turned")
                    for c in range(CH):
                        last = pe.transpose(tiles(B6)[:, c, :], dc[:, 2, c * P:(c + 1) * P], ident)
                    done(last, "v_turned")
                    for m, bank in enumerate((B7, B5)):
                        if m == 1:
                            act("exp_g")
                            dve("decay_min")
                        for n in range(2):
                            c = 2 * m + n
                            tok = slice(c * P, (c + 1) * P)
                            for part in (1, 0):
                                o = tiles(bank)[:, 2 * n + (1 - part), :]
                                last = mm(o, dc[:, 1, tok], dc[:, part, tok])
                        done(last, ("a01", "a23")[m])
                    dve("t0")
                    act("kg")
                    dve("kd")
                    for c in range(CH):
                        last = pe.transpose(tiles(B4)[:, c, :], tt[:, c, :], ident)
                    done(last, "inv0_turned")
                    for s in range(1, LEVELS):
                        dve(f"c{s}")
                        act("inv0" if s == 1 else f"p{s - 1}")
                        if s > 1:
                            dve(f"n{s - 1}")
                        for c in range(CH):
                            last = mm(tiles(B4)[:, c, :], tiles(tmp[1])[:, c, :], tiles(tmp[0])[:, c, :])
                        done(last, f"p{s}")
                        act(f"p{s}")
                        if s == 1:
                            act("vk")
                            dve("qk")
                        for c in range(CH):
                            last = mm(tiles(B6)[:, c, :], tiles(tmp[2])[:, c, :], tt[:, c, :])
                        done(last, f"qt{s}")
                        if s < LEVELS - 1:
                            for c in range(CH):
                                last = mm(tiles(B7)[:, c, :], tt[:, c, :], tiles(tmp[2])[:, c, :])
                            done(last, f"q{s}")
                    dve(f"t{LEVELS - 1}")
                    for c in range(CH):
                        last = mm(tiles(B4)[:, c, :], kg[:, c, :], tt[:, c, :])
                    done(last, "w")
                    act("w")
                    dve("q_dec")
                    for c in range(CH):
                        if c:
                            dve(f"s{c - 1}")
                        o = B6[:, 0:P]
                        last = mm(o, tt[:, c, :], vk[:, c, :], True, c == 0)
                        if c:
                            last = mm(o, tiles(tmp[2])[:, c, :], state[:, :], False, True)
                        done(last, f"v{c}")
                        dve(f"v{c}")
                        o = tiles(B5)[:, c, :]
                        if c:
                            mm(o, state[:, :], qd[:, c * P:(c + 1) * P], True, False)
                        done(mm(o, vn[:, :], qk[:, c, :], c == 0, True), f"o{c}")
                        if c < CH - 1:
                            done(mm(B7[:, 0:P], kd[:, c, :], vn[:, :]), f"s{c}")
                    act("o_sq")
                    done(mm(B4[0:32, :], row_of[:, 0, :], tmp[3][:, :]), "rms_sums")
                    dve("rms_rec")
                    done(mm(B7, ident[0:2, 0:1].broadcast_to([2, P]), tmp[0][0:2, :]), "rms_rows")

            def merge(l):
                with pe.Fori(0, KD // 4) as i:
                    for n in range(4):
                        for m in range(6):
                            t = 6 * n + m
                            was_n, was_m = (n, m - 4) if m >= 4 else (n - 1, m + 2)
                            if was_m < 3:
                                pe.wait_ge(freed_a.sem, freed_a.at(l, FREE_A["merge"] + 3 * was_n + was_m + 1) + i * 12)
                            else:
                                pe.wait_ge(freed_d.sem, freed_d.at(l, FREE_D["merge"] + 3 * was_n + was_m - 2) + i * 12)
                            o = acc[:, t % 4, :]
                            u = 5 * n + min(m, 3)
                            if m <= 3:
                                unit_here(l, i * 20 + (UNIT0["merge"] + u))
                            if m < 3:
                                last = unit(o, u % SLOTS, range(KD), 0, of_x, True, True)
                            elif m == 3:
                                last = unit(o, u % SLOTS, range(0, 4), 0, of_y, True, True)
                            elif m == 4:
                                last = unit(o, u % SLOTS, range(4, 8), 4, of_y, True, True, begins=False)
                            else:
                                unit_here(l, i * 20 + (UNIT0["merge"] + u + 1))
                                last = unit(o, (u + 1) % SLOTS, range(8, 12), 0, of_y, True, True)
                            last.then_inc(acc_ready.sem, 1)

            def of_y(k):
                if k < KB:
                    return yah[:, k, :], yal[:, k, :]
                return ych[:, k - KB, :], ycl[:, k - KB, :]

            def memory_kv(l):
                pe.wait_ge(freed_d.sem, freed_d.at(l, FREE_D["mix_out"] + KD))
                pe.wait_ge(mem_lo.sem, mem_lo.at(l, 1))
                for n in range(KD):
                    simple_tile(l, "mem_k", n, cols=slice(0, MEM), rhs=lambda k: (meh[:, k, :], mel[:, k, :]))
                for t in range(4):
                    free_bank(l, "mem_v", t - 3)
                for k in range(KD):
                    unit_here(l, UNIT0["mem_v"] + k)
                    for t in range(4):
                        tok = slice((t // 2) * P, (t // 2 + 1) * P)
                        c = slice((t % 2) * SEQ, (t % 2 + 1) * SEQ)
                        s = k % SLOTS
                        first = mm(acc[:, t, :], meh[:, k, tok], wh[:, s, c], k == 0, False)
                        if t == 0:
                            first.then_inc(unit_begun, 1)
                        mm(acc[:, t, :], meh[:, k, tok], wl[:, s, c], False, False)
                        last = mm(acc[:, t, :], mel[:, k, tok], wh[:, s, c], False, k == KD - 1)
                        if k == KD - 1:
                            last.then_inc(acc_ready.sem, 1)

            def cross_attention(l):
                with pe.Fori(0, 2) as i:
                    for n in range(4):
                        simple_tile(l, "x_q", n, x_ready(l, 2) if n == 0 else None, i=i)
                pe.wait_ge(freed_a.sem, freed_a.at(l, FREE_A["x_q"] + KD))

                def score(n):
                    h, i = divmod(n, CH)
                    if n >= 2:
                        pe.wait_ge(x_exps.sem, x_exps.at(l, n - 1))
                    for m in range(2):
                        last = mm(aux[:, n % 2, 0:MEM], xq[:, 2 * h + m, i * P:(i + 1) * P], xk[:, 2 * h + m, :], m == 0, m == 1)
                    last.then_inc(x_scores.sem, 1)

                def turn(n):
                    pe.wait_ge(x_probs.sem, x_probs.at(l, n + 1))
                    if n >= 2:
                        pe.wait_ge(x_turned_out.sem, x_turned_out.at(l, n - 1))
                    for j in range(KM):
                        last = pe.transpose(aux[:, 2 + n % 2, j * P:(j + 1) * P], x_sc(n)[:, j * P:(j + 1) * P], ident)
                    last.then_inc(x_turned.sem, 1)

                def values(h):
                    pe.wait_ge(x_turned_out.sem, x_turned_out.at(l, CH * (h + 1)))
                    for m in range(2):
                        if h:
                            pe.wait_ge(xo_lo.sem, xo_lo.at(l, 2 * h + m - 1))
                        for j in range(KM):
                            f = slice((2 * h + m) * P, (2 * h + m + 1) * P)
                            last = mm(acc[:, 2 + m, :], xv[:, j, f], tmp[2 + j][:, :], j == 0, j == KM - 1)
                        last.then_inc(x_att_out.sem, 1)

                score(0)
                score(1)
                for n in range(HX * CH):
                    turn(n)
                    if n + 2 < HX * CH:
                        score(n + 2)
                    if n % CH == CH - 1:
                        values(n // CH)

            pe.wait_ge(consts_set, 9)
            pe.wait_ge(const_loaded, 16)
            with pe.Fori(0, DEPTH) as l:
                ffn(l, 0, 0)
                attention(l)
                rg_lru(l)
                delta_rows(l)
                delta(l)
                pe.wait_ge(freed_a.sem, freed_a.at(l, FREE_A["delta"] + 4 * HN))
                wait_apart(pe, dn_dve.sem, dn_dve.after(l, HN - 1, "y_lo"))
                merge(l)
                pe.wait_ge(freed_a.sem, freed_a.at(l, FREE_A["merge"] + 3 * KD))
                out_projection(l, "mix_out", 1, one_unit(
                    l, "mix_out", lambda k: (mh[:, k, :], ml[:, k, :]),
                    lambda k: pe.wait_ge(merged_lo.sem, merged_lo.at(l, k + 1))))
                memory_kv(l)
                cross_attention(l)
                out_projection(l, "x_out", 2, one_unit(
                    l, "x_out", lambda k: (oh[:, k, :], ol[:, k, :]),
                    lambda k: pe.wait_ge(xo_lo.sem, xo_lo.at(l, k + 1))))
                ffn(l, 1, 3)

        HALF_STEP = 0.5 * 0.5 / ALPHA
        GATE_STEP = 0.5 / ALPHA
        GELU_IN = float(np.sqrt(2.0 / np.pi))

        @block.scalar
        def _(act):
            chain = Chain(act, act_step)

            def fn(out, in_, func, **kw):
                return act.activation(out, in_, func, **kw)

            def tile_ready(l, name, n):
                act.wait_ge(acc_ready.sem, acc_ready.at(l, TILE0[name] + 1) + n)

            def ffn_inner(l, which):
                up = f"ffn_up{which}"
                with act.Fori(0, KF // 2) as i:
                    for m in range(2):
                        tile_ready(l, up, i * 4 + 2 * m)
                        act.wait_ge(freed_d.sem, freed_d.at(l, FREE_D[up] + 2 * m) + i * 4)
                        fn(tmp[0][:, :], acc[:, 2 * m, :], ACT.Tanh, scale=0.5).then_inc(silu_th.sem, 1)
                        act.wait_ge(freed_d.sem, freed_d.at(l, FREE_D[up] + 2 * m + 2) + i * 4)
                        fn(hh[:, i * 2 + m, :], tmp[2][:, :], ACT.Copy).then_inc(inner_hi.sem, 1)

            def out_projection(l, name, norm):
                with act.Fori(0, KD // 4) as i:
                    for n in range(4):
                        d = i * 4 + n
                        act.wait_ge(freed_d.sem, freed_d.at(l, FREE_D[name] + 1) + d)
                        fn(xh[:, d, :], xf[:, d, :], ACT.Copy).then_inc(y_hi.sem, 1)
                        wait_apart(act, y_sq_lo.sem, y_sq_lo.at(l, norm * KD) + d)
                        fn(tmp[3][:, :], xf[:, d, :], ACT.Square).then_inc(y_sq.sem, 1)
                        act.wait_ge(y_sq.sem, y_sq.at(l, norm * KD + 1) + d)
                        act.wait_ge(stat_added.sem, stat_added.at(l, norm * KD) + d)
                        fn(sq_hi[:, :], tmp[3][:, :], ACT.Copy).then_inc(y_sq_hi.sem, 1)

            def layer_norm(l, norm):
                act.wait_ge(variance.sem, variance.at(l, norm + 1))
                fn(tmp[0][:, :], tmp[3][:, :], ACT.Sqrt, bias=eps_0[:, :]).then_inc(deviation.sem, 1)
                act.wait_ge(par_loaded, l * 16 + 16)
                for d in range(KD):
                    act.wait_ge(centred.sem, centred.at(l, norm * KD + d + 1))
                    c = norm * KD + d
                    fn(xf[:, d, :], xf[:, d, :], ACT.Identity, scale=par[:, P_LNG + c:P_LNG + c + 1],
                       bias=par[:, P_LNB + c:P_LNB + c + 1]).then_inc(affine.sem, 1)
                    act.wait_ge(affine.sem, affine.at(l, norm * KD + d + 1))
                    fn(xh[:, d, :], xf[:, d, :], ACT.Copy).then_inc(x_hi.sem, 1)

            def attention(l):
                for n in range(2 * KB):
                    tile_ready(l, "att_qk", n)
                    dst, scale = (aq[:, n, :], HDA ** -0.5) if n < KB else (ak[:, n - KB, :], 1.0)
                    fn(dst, acc[:, n % 4, :], ACT.Copy, scale=scale).then_inc(freed_a.sem, 1)
                for t in range(CH):
                    tile_ready(l, "att_v", t)
                    fn(av[:, t, :], acc[:, t, :], ACT.Copy).then_inc(freed_a.sem, 1)

                def turned_copy(n):
                    h, i = divmod(n, CH)
                    act.wait_ge(turned.sem, turned.at(l, n + 1))
                    act.wait_ge(att_out.sem, att_out.at(l, h))
                    fn(pt[:, 0:i + 1, i * P:(i + 1) * P], tiles(aux[:, 2 + n % 2, :])[:, 0:i + 1, :],
                       ACT.Copy).then_inc(turned_out.sem, 1)

                def out_copy(pair):
                    act.wait_ge(att_out.sem, att_out.at(l, 2 * pair + 2))
                    fn(ych[:, KB + pair, :], acc[:, pair % 2, :], ACT.Copy).then_inc(yc_hi.sem, 1)

                for n in range(HA * CH):
                    i = n % CH
                    act.wait_ge(row_max.sem, row_max.at(l, n + 1))
                    s = sc[:, i, 0:(i + 1) * P]
                    fn(s, s, ACT.Exp, bias=neg_max[:, n:n + 1], accum_out=row_sum[:, n:n + 1]).then_inc(exps.sem, 1)
                    if n >= 1:
                        turned_copy(n - 1)
                    if n >= 2 and (n - 1) % (2 * CH) == 0:
                        out_copy((n - 1) // (2 * CH) - 1)
                turned_copy(HA * CH - 1)
                out_copy(KB - 1)

            def rg_lru(l):
                def dve(step):
                    act.wait_ge(lru_dve.sem, lru_dve.after(l, 0, step))

                def own(step):
                    act.wait_ge(lru_act.sem, lru_act.after(l, 0, step))
                done = lru_act.done
                for p in range(KB):
                    tile_ready(l, "lru_x", p)
                    if p == 0:
                        act.dma_start(gate_w[:, :, :, :], gate_w_d[l]).then_inc(mix_par_loaded[0], 16)
                    fn(lx[:, p, 3:SEQ + 3], acc[:, p, :], ACT.Copy).then_inc(freed_a.sem, 1)
                for p in range(KB):
                    tile_ready(l, "lru_g", p)
                    fn(lg[:, p, :], acc[:, p, :], ACT.Copy).then_inc(freed_a.sem, 1)
                act.wait_ge(lam_arg.sem, lam_arg.at(l, 1))
                fn(lam[:, 2, :], lam[:, 1, :], ACT.Exp, scale=-1.0).then_inc(lam_exp.sem, 1)
                act.wait_ge(lam_ready.sem, lam_ready.at(l, 1))
                for p in range(KB):
                    for g, dst in enumerate((lr, li)):
                        act.wait_ge(lru_gates.sem, lru_gates.at(l, 2 * p + g + 1))
                        done(fn(dst[:, p, :], aux[:, 2 * (p % 2) + g, :], ACT.Tanh, scale=0.5,
                                bias=lam[:, 6 + g, p:p + 1]), f"{'ri'[g]}{p}")
                    own(f"r{p}")
                    done(fn(la[:, p, :], lr[:, p, :], ACT.Exp, scale=lam[:, 4, p:p + 1], bias=lam[:, 4, p:p + 1]), f"a{p}")
                    done(fn(lr[:, p, :], lr[:, p, :], ACT.Tanh, scale=lam[:, 5, p:p + 1], bias=lam[:, 5, p:p + 1]), f"s{p}")
                for p in range(KB):
                    dve(f"q{p}")
                    done(fn(lr[:, p, :], lr[:, p, :], ACT.Sqrt, scale=0.5, bias=eps_0[:, :]), f"q{p}")
                for p in range(KB):
                    if p == 0:
                        dve("h3")
                    done(fn(tmp[0][:, :], lg[:, p, :], ACT.Square), f"g_sq{p}")
                    dve(f"g_arg{p}")
                    done(fn(tmp[1][:, :], tmp[0][:, :], ACT.Tanh, scale=GELU_IN), f"g_th{p}")
                    dve(f"y{p}")
                    done(fn(ych[:, p, :], tmp[2][:, :], ACT.Copy), f"y_hi{p}")

            def delta_rows(l):
                act.wait_ge(lru_dve.sem, lru_dve.after(l, 0, "y_lo3"))
                act.dma_start(ba_w[:, :, :], ba_w_d[l]).then_inc(mix_par_loaded[1], 16)
                act.wait_ge(row_arg.sem, row_arg.at(l, 1))
                fn(tmp[1][0:HN, :], tmp[0][0:HN, :], ACT.Exp, scale=-1.0)
                fn(nea[0:HN, 0:1], par[0:HN, P_ALOG:P_ALOG + 1], ACT.Exp).then_inc(row_exp.sem, 1)
                fn(rows[32:32 + HN, :], B7[32:32 + HN, :], ACT.Tanh, scale=0.5).then_inc(beta_th.sem, 1)
                act.wait_ge(cols_ready.sem, cols_ready.at(l, 1))
                fn(cols[:, 2, :, :], cols[:, 0, :, :], ACT.Exp).then_inc(cols_exp.sem, 1)

            def delta(l):
                act.wait_ge(cols_exp.sem, cols_exp.at(l, 1))
                with act.Fori(0, HN) as h:
                    def dve(step):
                        act.wait_ge(dn_dve.sem, dn_dve.after(l, h, step))

                    def pe_(step):
                        act.wait_ge(dn_pe.sem, dn_pe.after(l, h, step))
                    done = dn_act.done
                    for m, dst in enumerate((dx[:, 0, 3:], dx[:, 1, 3:], dx[:, 2, 3:], dz[:, :])):
                        tile_ready(l, "delta", h * 4 + m)
                        fn(dst, acc[:, m, :], ACT.Copy).then_inc(freed_a.sem, 1)
                    for m in range(3):
                        dve(f"conv{m}")
                        done(fn(tmp[m][:, :], dc[:, m, :], ACT.Tanh, scale=0.5), f"th{m}")
                    for m, name in enumerate("qk"):
                        dve(f"silu{m}")
                        done(fn(tmp[m][:, :], dc[:, m, :], ACT.Square), f"sq_{name}")
                    pe_("norm_sums")
                    dve("silu2")
                    done(fn(tmp[2][0:32, :], B4[0:32, :], ACT.Sqrt, bias=eps_l2[0:32, :]), "norm_std")
                    pe_("decay_rows")
                    done(fn(eg[:, :], B5, ACT.Exp), "exp_g")
                    dve("decay_min")
                    done(fn(dt_[:, :, :], dt_[:, :, :], ACT.Exp), "decay_exp")
                    dve("kd_arg")
                    done(fn(hc[:, 1, :], hc[:, 1, :], ACT.Exp), "kd_exp")
                    done(fn(hc[:, 0, :], hc[:, 0, :], ACT.Exp), "last_exp")
                    pe_("k_turned")
                    for c in range(CH):
                        last = fn(kg[:, c, :], tiles(B4)[:, c, :], ACT.Identity, scale=cols[:, 2, c, bass.ds(h, 1)],
                                  bias=eps_0[:, :])
                    done(last, "kg")
                    pe_("v_turned")
                    done(fn(vk[:, :, :], tiles(B6), ACT.Copy, scale=0.5), "vk")
                    pe_("inv0_turned")
                    done(fn(tmp[0][:, :], B4, ACT.Copy), "inv0")
                    for s in range(1, LEVELS):
                        pe_(f"p{s}")
                        done(fn(tmp[2][:, :], B4, ACT.Copy), f"p{s}")
                    pe_("w")
                    done(fn(tmp[2][:, :], B4, ACT.Copy, scale=-1.0), "w")
                    pe_(f"o{CH - 1}")
                    done(fn(os_[:, :], B5, ACT.Copy, scale=0.5), "o")
                    done(fn(tmp[3][:, :], B5, ACT.Square), "o_sq")
                    pe_("rms_sums")
                    done(fn(tmp[1][0:32, :], B4[0:32, :], ACT.Sqrt, scale=1.0 / P, bias=eps_rms[0:32, :]), "rms_std")
                    done(fn(tmp[2][:, :], dz[:, :], ACT.Tanh, scale=0.5), "z_th")
                    dve("y")
                    done(fn(yah[:, h, :], tmp[2][:, :], ACT.Copy), "y_hi")

            def merge(l):
                with act.Fori(0, KD // 4) as i:
                    for n in range(4):
                        for r in range(NBR):
                            tile_ready(l, "merge", i * 24 + (6 * n + r))
                            fn(gt[:, 0, r, :], acc[:, (6 * n + r) % 4, :], ACT.Tanh, scale=0.5).then_inc(freed_a.sem, 1)
                        act.wait_ge(merged.sem, merged.at(l, n + 1) + i * 4)
                        fn(mh[:, i * 4 + n, :], tmp[0][:, :], ACT.Copy).then_inc(merged_hi.sem, 1)

            def memory_kv(l):
                act.wait_ge(mem_loaded, l * 16 + 16)
                fn(meh[:, :, :], mraw[:, :, :], ACT.Copy).then_inc(mem_hi.sem, 1)

            def memory_kv_out(l):
                for n in range(KD):
                    tile_ready(l, "mem_k", n)
                    fn(xk[:, n, :], acc[:, n % 4, 0:MEM], ACT.Copy).then_inc(freed_a.sem, 1)
                for t in range(4):
                    tile_ready(l, "mem_v", t)
                    fn(xv[:, t // 2, (t % 2) * SEQ:(t % 2 + 1) * SEQ], acc[:, t, :], ACT.Copy).then_inc(freed_a.sem, 1)

            def cross_attention(l):
                with act.Fori(0, 2) as i:
                    for n in range(4):
                        tile_ready(l, "x_q", i * 4 + n)
                        fn(xq[:, i * 4 + n, :], acc[:, n, :], ACT.Copy, scale=(DM // HX) ** -0.5).then_inc(freed_a.sem, 1)

                def turned_copy(n):
                    h, i = divmod(n, CH)
                    act.wait_ge(x_turned.sem, x_turned.at(l, n + 1))
                    act.wait_ge(x_att_out.sem, x_att_out.at(l, 2 * h))
                    for j in range(KM):
                        last = fn(tmp[2 + j][:, i * P:(i + 1) * P], aux[:, 2 + n % 2, j * P:(j + 1) * P], ACT.Copy)
                    last.then_inc(x_turned_out.sem, 1)

                def out_copy(h):
                    for m in range(2):
                        act.wait_ge(x_att_out.sem, x_att_out.at(l, 2 * h + m + 1))
                        fn(oh[:, 2 * h + m, :], acc[:, 2 + m, :], ACT.Copy).then_inc(xo_hi.sem, 1)

                for n in range(HX * CH):
                    act.wait_ge(x_row_max.sem, x_row_max.at(l, n + 1))
                    if n >= 4:
                        act.wait_ge(x_turned.sem, x_turned.at(l, n - 3))
                    fn(x_sc(n), aux[:, n % 2, 0:MEM], ACT.Exp, bias=x_negmax[:, n:n + 1],
                       accum_out=x_sum[:, n:n + 1]).then_inc(x_exps.sem, 1)
                    if n >= 1:
                        turned_copy(n - 1)
                    if n >= 2 and (n - 1) % CH == 0:
                        out_copy((n - 1) // CH - 1)
                turned_copy(HX * CH - 1)
                out_copy(HX - 1)

            act.sem_inc(freed_a.sem, 4)
            act.wait_ge(x_loaded, 16)
            for k in range(KD):
                fn(xh[:, k, :], xf[:, k, :], ACT.Copy).then_inc(x_hi.sem, 1)
            with act.Fori(0, DEPTH) as l:
                act.wait_ge(x_hi.sem, x_hi.at(l, 0))
                act.dma_start(par[:, :], par_d[l]).then_inc(par_loaded, 16)
                ffn_inner(l, 0)
                out_projection(l, "ffn_down0", 0)
                act.wait_ge(stat_added.sem, stat_added.at(l, KD))
                act.dma_start(ext[:, P - 1:3 * P - 1], table_d[l][:, 0:2 * P]).then_inc(mix_par_loaded[2], 16)
                layer_norm(l, 0)
                act.wait_ge(ext_padded.sem, ext_padded.at(l, 1))
                act.dma_start(ext_d, ext[:, :]).then_inc(ext_stored, 16)
                act.wait_ge(ext_stored, l * 16 + 16)
                act.dma_start(bias[:, :, :], bass.AP(tensor=ext_d.tensor, offset=0,
                                                     ap=[[1, P], [3 * P - 1, HA], [1, 2 * P]])).then_inc(bias_loaded, 16)
                attention(l)
                rg_lru(l)
                delta_rows(l)
                delta(l)
                merge(l)
                out_projection(l, "mix_out", 1)
                act.wait_ge(stat_added.sem, stat_added.at(l, 2 * KD))
                act.dma_start(mraw[:, :, :], memT.rearrange("(k p) t -> p k t", p=P)).then_inc(mem_loaded, 16)
                memory_kv(l)
                layer_norm(l, 1)
                memory_kv_out(l)
                cross_attention(l)
                out_projection(l, "x_out", 2)
                layer_norm(l, 2)
                ffn_inner(l, 1)
                out_projection(l, "ffn_down1", 3)
                layer_norm(l, 3)

        @block.vector
        def _(dve):
            chain = Chain(dve, dve_step)
            link = chain.link
            tt_, ts_, stt_ = dve.tensor_tensor, dve.tensor_scalar, dve.scalar_tensor_tensor

            def tile_ready(l, name, n):
                dve.wait_ge(acc_ready.sem, acc_ready.at(l, TILE0[name] + 1) + n)

            def low(dst, whole, high):
                return tt_(dst, whole, high.bitcast(F32), ALU.subtract)

            def ffn_inner(l, which):
                up = f"ffn_up{which}"
                with dve.Fori(0, KF // 2) as i:
                    for m in range(2):
                        j = i * 2 + m
                        dve.wait_ge(silu_th.sem, silu_th.at(l, which * KF + 1) + j)
                        stt_(tmp[1][:, :], tmp[0][:, :], 1.0, acc[:, 2 * m, :], ALU.add, ALU.mult).then_inc(freed_d.sem, 1)
                        dve.wait_ge(freed_d.sem, freed_d.at(l, FREE_D[up] + 2 * m + 1) + i * 4)
                        tile_ready(l, up, i * 4 + (2 * m + 1))
                        tt_(tmp[2][:, :], tmp[1][:, :], acc[:, 2 * m + 1, :], ALU.mult).then_inc(freed_d.sem, 1)
                        dve.wait_ge(inner_hi.sem, inner_hi.at(l, which * KF + 1) + j)
                        low(hl[:, j, :], tmp[2][:, :], hh[:, j, :]).then_inc(inner_lo.sem, 1)

            def out_projection(l, name, norm, factor):
                with dve.Fori(0, KD // 4) as i:
                    for n in range(4):
                        d = i * 4 + n
                        tile_ready(l, name, d)
                        stt_(xf[:, d, :], acc[:, n, :], factor, xf[:, d, :], ALU.mult, ALU.add).then_inc(freed_d.sem, 1)
                        dve.wait_ge(y_hi.sem, y_hi.at(l, norm * KD + 1) + d)
                        low(xl[:, d, :], xf[:, d, :], xh[:, d, :]).then_inc(y_lo.sem, 1)
                        dve.wait_ge(y_sq_hi.sem, y_sq_hi.at(l, norm * KD + 1) + d)
                        low(sq_lo[:, :], tmp[3][:, :], sq_hi[:, :]).then_inc(y_sq_lo.sem, 1)

            def layer_norm(l, norm):
                dve.wait_ge(stat_added.sem, stat_added.at(l, (norm + 1) * KD))
                link(dve.tensor_copy(tmp[1][:, :], B4))
                link(tt_(tmp[2][:, :], tmp[1][:, :], tmp[1][:, :], ALU.mult))
                link(stt_(tmp[3][:, :], tmp[2][:, :], -1.0, B5, ALU.mult, ALU.add))
                ts_(tmp[3][:, :], tmp[3][:, :], 0.0, LN_EPS / ALPHA ** 2, ALU.max, ALU.add).then_inc(variance.sem, 1)
                dve.wait_ge(deviation.sem, deviation.at(l, norm + 1))
                link(dve.reciprocal(tmp[0][:, :], tmp[0][:, :]))
                link(tt_(tmp[1][:, :], tmp[1][:, :], tmp[0][:, :], ALU.mult))

                def split(d):
                    dve.wait_ge(x_hi.sem, x_hi.at(l, norm * KD + d + 1))
                    low(xl[:, d, :], xf[:, d, :], xh[:, d, :]).then_inc(x_lo.sem, 1)

                for d in range(KD):
                    link(tt_(xf[:, d, :], xf[:, d, :], tmp[0][:, :], ALU.mult))
                    tt_(xf[:, d, :], xf[:, d, :], tmp[1][:, :], ALU.subtract).then_inc(centred.sem, 1)
                    if d >= 1:
                        split(d - 1)
                split(KD - 1)

            def softplus(out, x, e, t, u, n_rows):
                link(ts_(t, e, 2.0, None, ALU.add))
                link(dve.reciprocal(t, t))
                link(tt_(t, e, t, ALU.mult))
                link(tt_(u, t, t, ALU.mult))
                link(ts_(e, u, 1.0 / 15, None, ALU.mult))
                for k in range(6, 0, -1):
                    link(stt_(e, e, 1.0 / (2 * k + 1), u, ALU.add, ALU.mult))
                link(stt_(e, e, 1.0, t, ALU.add, ALU.mult))
                link(ts_(out, x, 0.0, None, ALU.max))
                return stt_(out, e, 2.0, out, ALU.mult, ALU.add)

            def attention(l):
                dve.wait_ge(mix_par_loaded[2], l * 16 + 16)
                dve.tensor_copy(ext[:, 0:P - 1], ext[:, P - 1:P].broadcast_to([HA, P - 1])).then_inc(ext_padded.sem, 1)
                for m in range(4):
                    dve.wait_ge(bias_flipped.sem, bias_flipped.at(l, 4))
                    dve.tensor_copy(bias[:, 2 * m:2 * m + 2, :], aux[:, m, :].rearrange("p (h k) -> p h k", h=2)).then_inc(bias_copied.sem, 1)
                dve.wait_ge(bias_copied.sem, bias_copied.at(l, 4))
                dve.memset(bias[0:P // 2, :, 3 * P // 2:2 * P], NEG).then_inc(bias_masked.sem, 1)
                dve.wait_ge(bias_masked.sem, bias_masked.at(l, 1))

                def normalise(n):
                    s = sc[:, n % CH, 0:(n % CH + 1) * P]
                    dve.wait_ge(exps.sem, exps.at(l, n + 1))
                    link(dve.reciprocal(inv_sum[:, n:n + 1], row_sum[:, n:n + 1]))
                    ts_(s, s, inv_sum[:, n:n + 1], None, ALU.mult).then_inc(probs.sem, 1)

                def out_low(pair):
                    dve.wait_ge(yc_hi.sem, yc_hi.at(l, pair + 1))
                    low(ycl[:, KB + pair, :], acc[:, pair % 2, :], ych[:, KB + pair, :]).then_inc(yc_lo.sem, 1)

                for n in range(HA * CH):
                    h, i = divmod(n, CH)
                    bank = aux[:, n % 2, :]
                    if n >= CH:
                        dve.wait_ge(turned.sem, turned.at(l, n - CH + 1))
                    dve.wait_ge(scores.sem, scores.at(l, n + 1))
                    if i >= 2:
                        far = slice(0, (i - 1) * P)
                        ts_(sc[:, i, far], bank[:, far], bias[:, h, 0:1], None, ALU.add)
                    near = slice(max(i - 1, 0) * P, (i + 1) * P)
                    tt_(sc[:, i, near], bank[:, near], bias[:, h, (0 if i else P):2 * P], ALU.add).then_inc(biased.sem, 1)
                    dve.wait_ge(biased.sem, biased.at(l, n + 1))
                    dve.tensor_reduce(neg_max[:, n:n + 1], sc[:, i, 0:(i + 1) * P], AX.X, ALU.max, negate=True).then_inc(row_max.sem, 1)
                    if n >= 1:
                        normalise(n - 1)
                    if n >= 2 and (n - 1) % (2 * CH) == 0:
                        out_low((n - 1) // (2 * CH) - 1)
                normalise(HA * CH - 1)
                out_low(KB - 1)

            def conv(dst, src, weight, add=None):
                if add is None:
                    link(ts_(dst, src[:, 0:SEQ], weight(0), None, ALU.mult))
                else:
                    link(ts_(dst, src[:, 0:SEQ], weight(0), add, ALU.mult, ALU.add))
                for tap in (1, 2):
                    link(stt_(dst, src[:, tap:SEQ + tap], weight(tap), dst, ALU.mult, ALU.add))
                return stt_(dst, src[:, 3:SEQ + 3], weight(3), dst, ALU.mult, ALU.add)

            def rg_lru(l):
                def act_(step):
                    dve.wait_ge(lru_act.sem, lru_act.after(l, 0, step))
                done = lru_dve.done

                def own(step):
                    dve.wait_ge(lru_dve.sem, lru_dve.after(l, 0, step))

                def col(c):
                    return par[:, c:c + 1]
                tile_ready(l, "lru_x", 0)
                link(dve.memset(lx[:, :, 0:3], 0.0))
                lam_p = par[:, P_LAM:P_LAM + KB]
                link(ts_(lam[:, 0, :], lam_p, -1.0, None, ALU.mult))
                tt_(lam[:, 1, :], lam[:, 0, :], lam_p, ALU.max).then_inc(lam_arg.sem, 1)
                link(ts_(lam[:, 6:8, :], par[:, P_GB:P_GB + 2 * KB].rearrange("p (g k) -> p g k", g=2), 0.5, None, ALU.mult))
                for p in range(KB):
                    dve.wait_ge(freed_a.sem, freed_a.at(l, FREE_A["lru_x"] + p + 1))
                    done(conv(lc[:, p, :], lx[:, p, :], lambda tap: col(P_LCW + 4 * p + tap), col(P_LCB + p)), f"conv{p}")
                dve.wait_ge(lam_exp.sem, lam_exp.at(l, 1))
                link(softplus(lam[:, 5, :], lam[:, 0, :], lam[:, 2, :], lam[:, 3, :], lam[:, 4, :], P))
                link(ts_(lam[:, 4, :], lam[:, 5, :], -LRU_C / 2, None, ALU.mult))
                ts_(lam[:, 5, :], lam[:, 5, :], LRU_C / 2, None, ALU.mult).then_inc(lam_ready.sem, 1)
                for p in range(KB):
                    act_(f"s{p}")
                    if p:
                        own(f"q{p - 1}")
                    link(ts_(tmp[0][:, :], lr[:, p, :], 1.0, None, ALU.add))
                    link(dve.reciprocal(tmp[0][:, :], tmp[0][:, :]))
                    done(tt_(lr[:, p, :], lr[:, p, :], tmp[0][:, :], ALU.mult), f"q{p}")
                    done(stt_(li[:, p, :], li[:, p, :], 1.0, lc[:, p, :], ALU.add, ALU.mult), f"xi{p}")
                for p in range(KB):
                    act_(f"q{p}")
                    link(tt_(li[:, p, :], li[:, p, :], lr[:, p, :], ALU.mult))
                    done(dve.tensor_tensor_scan(lc[:, p, :], la[:, p, :], li[:, p, :], 0.0, ALU.mult, ALU.add), f"h{p}")
                for p in range(KB):
                    act_(f"g_sq{p}")
                    link(ts_(tmp[0][:, :], tmp[0][:, :], 0.044715, 1.0, ALU.mult, ALU.add))
                    done(tt_(tmp[0][:, :], tmp[0][:, :], lg[:, p, :], ALU.mult), f"g_arg{p}")
                    act_(f"g_th{p}")
                    link(stt_(tmp[1][:, :], tmp[1][:, :], 1.0, lg[:, p, :], ALU.add, ALU.mult))
                    done(stt_(tmp[2][:, :], lc[:, p, :], 0.5, tmp[1][:, :], ALU.mult, ALU.mult), f"y{p}")
                    act_(f"y_hi{p}")
                    done(low(ycl[:, p, :], tmp[2][:, :], ych[:, p, :]), f"y_lo{p}")
                    own(f"y_lo{p}")

            def delta_rows(l):
                link(dve.memset(rows[:, :], 0.0))
                link(dve.memset(dx[:, :, 0:3], 0.0))
                r = slice(0, HN)
                dve.wait_ge(ba_ready.sem, ba_ready.at(l, 1))
                link(ts_(grow[r, :], B7[r, :], par[r, P_DT:P_DT + 1], None, ALU.add))
                link(ts_(tmp[0][r, :], grow[r, :], -1.0, None, ALU.mult))
                tt_(tmp[0][r, :], tmp[0][r, :], grow[r, :], ALU.max).then_inc(row_arg.sem, 1)
                dve.wait_ge(row_exp.sem, row_exp.at(l, 1))
                link(softplus(grow[r, :], grow[r, :], tmp[1][r, :], tmp[2][r, :], tmp[3][r, :], HN))
                link(ts_(nea[r, 1:2], nea[r, 0:1], -1.0, None, ALU.mult))
                link(ts_(grow[r, :], grow[r, :], nea[r, 1:2], None, ALU.mult))
                for c in range(CH):
                    tok = slice(c * P, (c + 1) * P)
                    link(dve.tensor_tensor_scan(rows[r, tok], ones[r, :], grow[r, tok], 0.0, ALU.mult, ALU.add))
                dve.wait_ge(beta_th.sem, beta_th.at(l, 1))
                b = slice(32, 32 + HN)
                ts_(rows[b, :], rows[b, :], 0.5, 0.5, ALU.mult, ALU.add).then_inc(rows_ready.sem, 1)
                dve.wait_ge(rows_turned.sem, rows_turned.at(l, 1))
                link(dve.tensor_copy(cols[:, 1, :, :], tiles(B6)[:, :, 32:32 + HN]))
                dve.tensor_copy(cols[:, 0, :, :], tiles(B6)[:, :, 0:HN]).then_inc(cols_ready.sem, 1)

            def delta(l):
                wait_apart(dve, cols_ready.sem, cols_ready.at(l, 1))
                with chain.loop(HN, DELTA_LINKS) as h:
                    def act_(step):
                        dve.wait_ge(dn_act.sem, dn_act.after(l, h, step))

                    def pe_(step):
                        dve.wait_ge(dn_pe.sem, dn_pe.after(l, h, step))

                    def own(step):
                        dve.wait_ge(dn_dve.sem, dn_dve.after(l, h, step))
                    done = dn_dve.done

                    def wide(x):
                        return x.rearrange("p (a b) -> p a b", a=1).broadcast_to([P, CH, P])
                    for m in range(3):
                        dve.wait_ge(freed_a.sem, freed_a.at(l, FREE_A["delta"] + m + 1) + h * 4)
                        done(conv(dc[:, m, :], dx[:, m, :], lambda tap: par[:, bass.ds(h * 12 + (P_CW + 4 * m + tap), 1)]), f"conv{m}")
                    for m in range(3):
                        act_(f"th{m}")
                        done(stt_(dc[:, m, :], tmp[m][:, :], 1.0, dc[:, m, :], ALU.add, ALU.mult), f"silu{m}")
                    done(ts_(grow[0:HN, :], rows[0:HN, :], const[0:HN, bass.ds(h, 1)], None, ALU.mult), "g_row")
                    act_("norm_std")
                    done(dve.reciprocal(tmp[3][0:32, :], tmp[2][0:32, :]), "norm_rec")
                    pe_("norm_q")
                    done(stt_(dc[:, 0, :], dc[:, 0, :], float(P) ** -0.5, B6, ALU.mult, ALU.mult), "q_normed")
                    pe_("norm_k")
                    done(tt_(dc[:, 1, :], dc[:, 1, :], B7, ALU.mult), "k_normed")
                    act_("exp_g")
                    done(dve.tensor_copy(hc[:, 0, :].rearrange("p (c a) -> p c a", a=1), tiles(B5)[:, :, P - 1:P]), "g_last")
                    for c in range(CH):
                        last = ts_(dt_[:, c, :], tiles(B5)[:, c, :], cols[:, 0, c, bass.ds(h, 1)], 0.0, ALU.subtract, ALU.min)
                    done(last, "decay_min")
                    own("g_last")
                    done(tt_(hc[:, 1, :].rearrange("p (c a) -> p c a", a=1), hc[:, 0, :].rearrange("p (c a) -> p c a", a=1),
                             cols[:, 0, :, bass.ds(h, 1)], ALU.subtract), "kd_arg")
                    act_("exp_g")
                    done(tt_(qd[:, :], dc[:, 0, :], eg[:, :], ALU.mult), "q_dec")
                    act_("decay_exp")
                    done(tt_(dt_[:, :, :], dt_[:, :, :], wide(causal), ALU.mult), "decay")
                    act_("kg")
                    for c in range(CH):
                        last = ts_(kd[:, c, :], tiles(B4)[:, c, :], hc[:, 1, c:c + 1], None, ALU.mult)
                    done(last, "kd")
                    own("decay")
                    pe_("a01")
                    pe_("a23")
                    for part in range(2):
                        for c in range(CH):
                            o = tiles((B7, B5)[c // 2])[:, 2 * (c % 2) + part, :]
                            if part == 0:
                                last = stt_(mt[:, c, :], o, cols[:, 1, c, bass.ds(h, 1)], dt_[:, c, :], ALU.mult, ALU.mult)
                            else:
                                last = tt_(qk[:, c, :], o, dt_[:, c, :], ALU.mult)
                        done(last, ("m", "qk")[part])
                    own("m")
                    done(tt_(tiles(tmp[1]), mt[:, :, :], level_mask(0), ALU.mult), "c0")
                    own("c0")
                    done(tt_(tt[:, :, :], wide(ident), tiles(tmp[1]), ALU.subtract), "t0")
                    for s in range(1, LEVELS):
                        if s == 1:
                            own("t0")
                        done(tt_(tiles(tmp[1]), mt[:, :, :], level_mask(s), ALU.mult), f"c{s}")
                        pe_(f"q{s}" if s < LEVELS - 1 else f"qt{s}")
                        done(tt_(tt[:, :, :], tt[:, :, :], tiles(B6), ALU.subtract), f"t{s}")
                        if s < LEVELS - 1:
                            done(tt_(tmp[0][:, :], tmp[0][:, :], B7, ALU.subtract), f"n{s}")
                    for c in range(CH):
                        pe_(f"v{c}")
                        done(ts_(vn[:, :], B6[:, 0:P], cols[:, 1, c, bass.ds(h, 1)], None, ALU.mult), f"v{c}")
                        if c < CH - 1:
                            pe_(f"s{c}")
                            if c == 0:
                                done(dve.tensor_copy(state[:, :], B7[:, 0:P]), "s0")
                            else:
                                act_("last_exp")
                                done(stt_(state[:, :], state[:, :], hc[:, 0, c:c + 1], B7[:, 0:P], ALU.mult, ALU.add), f"s{c}")
                    act_("rms_std")
                    done(dve.reciprocal(tmp[0][0:32, :], tmp[1][0:32, :]), "rms_rec")
                    pe_("rms_rows")
                    done(tt_(os_[:, :], os_[:, :], B7, ALU.mult), "o_normed")
                    act_("z_th")
                    done(stt_(tmp[2][:, :], tmp[2][:, :], 1.0, dz[:, :], ALU.add, ALU.mult), "z_gate")
                    own("z_gate")
                    done(stt_(tmp[2][:, :], tmp[2][:, :], par[:, P_NW:P_NW + 1], os_[:, :], ALU.mult, ALU.mult), "y")
                    act_("y_hi")
                    done(low(yal[:, h, :], tmp[2][:, :], yah[:, h, :]), "y_lo")

            def merge(l):
                with chain.loop(KD // 4, MERGE_LINKS) as i:
                    for n in range(4):
                        for r in range(NBR):
                            dve.wait_ge(freed_a.sem, freed_a.at(l, FREE_A["merge"] + 3 * n + r + 1) + i * 12)
                            tile_ready(l, "merge", i * 24 + (6 * n + 3 + r))
                            stt_(tmp[r][:, :], gt[:, 0, r, :], 1.0, acc[:, (6 * n + 3 + r) % 4, :], ALU.add,
                                 ALU.mult).then_inc(freed_d.sem, 1)
                        dve.wait_ge(freed_d.sem, freed_d.at(l, FREE_D["merge"] + 3 * n + 3) + i * 12)
                        link(tt_(tmp[0][:, :], tmp[0][:, :], tmp[1][:, :], ALU.add))
                        tt_(tmp[0][:, :], tmp[0][:, :], tmp[2][:, :], ALU.add).then_inc(merged.sem, 1)
                        dve.wait_ge(merged_hi.sem, merged_hi.at(l, n + 1) + i * 4)
                        low(ml[:, i * 4 + n, :], tmp[0][:, :], mh[:, i * 4 + n, :]).then_inc(merged_lo.sem, 1)
                        dve.wait_ge(merged_lo.sem, merged_lo.at(l, n + 1) + i * 4)

            def cross_attention(l):
                def normalise(n):
                    dve.wait_ge(x_exps.sem, x_exps.at(l, n + 1))
                    link(dve.reciprocal(x_inv[:, n:n + 1], x_sum[:, n:n + 1]))
                    ts_(x_sc(n), x_sc(n), x_inv[:, n:n + 1], None, ALU.mult).then_inc(x_probs.sem, 1)

                def out_low(h):
                    for m in range(2):
                        dve.wait_ge(xo_hi.sem, xo_hi.at(l, 2 * h + m + 1))
                        low(ol[:, 2 * h + m, :], acc[:, 2 + m, :], oh[:, 2 * h + m, :]).then_inc(xo_lo.sem, 1)

                for n in range(HX * CH):
                    dve.wait_ge(x_scores.sem, x_scores.at(l, n + 1))
                    dve.tensor_reduce(x_negmax[:, n:n + 1], aux[:, n % 2, 0:MEM], AX.X, ALU.max, negate=True).then_inc(x_row_max.sem, 1)
                    if n >= 1:
                        normalise(n - 1)
                    if n >= 2 and (n - 1) % CH == 0:
                        out_low((n - 1) // CH - 1)
                normalise(HX * CH - 1)
                out_low(HX - 1)

            dve.sem_inc(freed_d.sem, 4)
            dve.wait_ge(consts_set, 9)
            dve.wait_ge(const_loaded, 16)
            for k in range(KD):
                dve.wait_ge(x_hi.sem, k + 1)
                low(xl[:, k, :], xf[:, k, :], xh[:, k, :]).then_inc(x_lo.sem, 1)
            with chain.loop(DEPTH, LAYER_LINKS) as l:
                ffn_inner(l, 0)
                out_projection(l, "ffn_down0", 0, HALF_STEP)
                layer_norm(l, 0)
                dve.wait_ge(par_loaded, l * 16 + 16)
                attention(l)
                rg_lru(l)
                delta_rows(l)
                delta(l)
                merge(l)
                out_projection(l, "mix_out", 1, GATE_STEP)
                dve.wait_ge(mem_hi.sem, mem_hi.at(l, 1))
                low(mel[:, :, :], mraw[:, :, :], meh[:, :, :]).then_inc(mem_lo.sem, 1)
                layer_norm(l, 1)
                cross_attention(l)
                out_projection(l, "x_out", 2, 1.0 / ALPHA)
                layer_norm(l, 2)
                ffn_inner(l, 1)
                out_projection(l, "ffn_down1", 3, HALF_STEP)
                layer_norm(l, 3)


def pack(x, mem, ln_g, ln_b, ffn_w12, ffn_w3, mix_w_in, dn_conv_w, dn_a_log, dn_dt_bias, dn_norm_w, lru_conv_w,
         lru_conv_b, lru_gate_w, lru_gate_b, lru_lambda, la_rel_bias, w_branch, mix_w_out, xa_wq, xa_wkv, xa_wo):
    A = np.asarray

    def stationary(w):
        k, m = w.shape
        return w.reshape(k // P, P, m // P, P).transpose(2, 1, 0, 3).reshape(m // P, P, -1)

    def padded(u, columns):
        out = np.zeros(u.shape[:-1] + (columns,), u.dtype)
        out[..., :u.shape[-1]] = u
        return out

    def units(w):
        n = -(-w.shape[-1] // UNIT)
        return padded(w, n * UNIT).reshape(len(w), P, n, UNIT).transpose(0, 2, 1, 3).reshape(-1, P, UNIT)

    def moving(w):
        k, m = w.shape
        per = UNIT // m
        return w.reshape(k // P // per, per, P, m).transpose(0, 2, 1, 3).reshape(-1, P, UNIT)

    q, kk, v, z, bb, aa, lx_, lg_, aq_, ak_, av_, gl = np.split(
        np.arange(mix_w_in.shape[2]), np.cumsum([BRW] * 4 + [HN] * 2 + [BRW] * 5))
    stream, par, ba, gw = [], [], [], []
    for l in range(DEPTH):
        w_in = A(mix_w_in[l])

        def cols_of(idx):
            return stationary(w_in[:, idx])

        def ffn(n):
            up = stationary(A(ffn_w12[l, n]))
            return [up.reshape(2, KF, P, UNIT).transpose(1, 0, 2, 3).reshape(-1, P, UNIT),
                    units(stationary(A(ffn_w3[l, n])))]
        stream += ffn(0)
        stream += [cols_of(aq_), cols_of(ak_), moving(w_in[:, av_]), cols_of(lx_), cols_of(lg_)]
        stream.append(np.stack([cols_of(i) for i in (q, kk, v, z)], 1).reshape(-1, P, UNIT))
        gates = cols_of(gl).reshape(NBR, KD, P, UNIT).transpose(1, 0, 2, 3)
        branch = units(stationary(A(w_branch[l]).reshape(NBR * BRW, DM))).reshape(KD, 2, P, UNIT)
        stream.append(np.concatenate([gates, branch], 1).reshape(-1, P, UNIT))
        stream += [stationary(A(mix_w_out[l])), stationary(A(xa_wkv[l])[:, :DM]), moving(A(xa_wkv[l])[:, DM:]),
                   stationary(A(xa_wq[l])), stationary(A(xa_wo[l]))]
        stream += ffn(1)

        def by_tile(a, n):
            return A(a).reshape(n, P).T
        cw = A(dn_conv_w[l]).reshape(4, 3, HN, P).transpose(3, 2, 1, 0).reshape(P, -1)
        lcw = A(lru_conv_w[l]).reshape(4, KB, P).transpose(2, 1, 0).reshape(P, -1)

        def rows(a):
            out = np.zeros((P, 1), np.float32)
            out[:HN, 0] = A(a)
            return out
        par.append(np.concatenate([
            by_tile(ln_g[l], 4 * KD), by_tile(ln_b[l], 4 * KD), cw, lcw, by_tile(lru_conv_b[l], KB),
            by_tile(lru_gate_b[l], 2 * KB), by_tile(lru_lambda[l], KB), A(dn_norm_w[l])[:, None],
            rows(dn_a_log[l]), rows(dn_dt_bias[l])], 1))
        b = np.zeros((P, KD, 64), np.float32)
        b[:, :, 0:HN] = w_in[:, aa].reshape(KD, P, HN).transpose(1, 0, 2)
        b[:, :, 32:32 + HN] = w_in[:, bb].reshape(KD, P, HN).transpose(1, 0, 2)
        ba.append(b)
        g = np.zeros((P, 2, KB, P), np.float32)
        for n in range(2 * KB):
            half = slice(64 * (n % 2), 64 * (n % 2) + 64)
            g[half, :, n // 2, half] = A(lru_gate_w[l])[:, n].transpose(1, 0, 2)
        gw.append(g)
    i = np.arange(P)
    const = [np.eye(P), i[:, None] <= i[None, :], np.eye(P)[::-1]]
    for s in range(LEVELS):
        b = 1 << s
        const.append((i[:, None] // b % 2 == 0) & (i[None, :] // b == i[:, None] // b + 1))
    return {"in_xT": np.ascontiguousarray(A(x)[0].T), "in_memT": np.ascontiguousarray(A(mem)[0].T),
            "in_stream": np.concatenate(stream, 0), "in_par": np.stack(par), "in_ba_w": np.stack(ba),
            "in_gate_w": np.stack(gw), "in_table": A(la_rel_bias), "in_const": np.concatenate(const, 1).astype(np.float32)}


def kernel(**inputs):
    import concourse.bacc as bacc
    from concourse.bass_utils import run_bass_kernel_spmd

    nc = bacc.Bacc("TRN2", target_bir_lowering=False, num_devices=1)
    arrays = pack(**inputs)
    ins = {n: nc.dram_tensor(n, a.shape, mybir.dt.from_np(a.dtype), kind="ExternalInput").ap() for n, a in arrays.items()}
    ext_d = nc.dram_tensor("rel_scratch", (HA, 3 * P - 1), F32).ap()
    out = nc.dram_tensor("out_xT", (DM, SEQ), F32, kind="ExternalOutput").ap()
    trunk(nc, ins["in_xT"], ins["in_memT"], ins["in_stream"], ins["in_par"], ins["in_ba_w"], ins["in_gate_w"],
          ins["in_table"], ins["in_const"], ext_d, out)
    got = run_bass_kernel_spmd(nc, [arrays], core_ids=[0]).results[0]["out_xT"]
    return np.ascontiguousarray(got.T)[None]
```

```python
from contextlib import ExitStack, contextmanager

import numpy as np

import concourse.bass as bass
from concourse import mybir

F32 = mybir.dt.float32
F32R = mybir.dt.float32r
ALU = mybir.AluOpType
ACT = mybir.ActivationFunctionType
AX = mybir.AxisListType

P = 128
DEPTH = 2
SEQ = 512
DM = 1024
KD = DM // P
FF = 2816
KF = FF // P
BRW = 512
KB = BRW // P
NBR = 3
HA = 8
HDA = 64
HX = 4
MEM = 256
KM = MEM // P
HN = 4
CH = SEQ // P
REL = 128
ALPHA = (2 * DEPTH) ** 0.25
LN_EPS = 1e-5
NORM_EPS = 1e-6
NEG = -1e30
LRU_C = 8.0
LAYER_LINKS = 225

UNIT = 1024
SLOTS = 4
LEVELS = 7

PHASES = [("ffn_up0", 2 * KF, 2 * KF), ("ffn_down0", KD, 3 * KD), ("att_qk", 2 * KB, 2 * KB),
          ("att_v", CH, CH), ("lru_x", KB, KB), ("lru_g", KB, KB), ("mixer", 16 * HN, 13 * HN), ("mix_out", KD, KD), ("mem_k", KD, KD), ("mem_v", 4, KD),
          ("x_q", KD, KD), ("x_out", KD, KD), ("ffn_up1", 2 * KF, 2 * KF), ("ffn_down1", KD, 3 * KD)]
TILE0, UNIT0 = {}, {}
_t = _u = 0
for _name, _tiles, _units in PHASES:
    TILE0[_name], UNIT0[_name] = _t, _u
    _t, _u = _t + _tiles, _u + _units
TILES, UNITS = _t, _u



def mixer_tiles():
    tiles, unit = [], 0

    def add(kind, a, b, at=0, ends=True):
        nonlocal unit
        tiles.append((kind, a, b, unit, at))
        unit += ends

    for m in range(4):
        add("proj", 0, m)
    for h in range(HN):
        for d in (2 * h, 2 * h + 1):
            add("gate", 1, d)
            add("gate", 2, d)
            add("up", 1, d, 0, ends=False)
            add("up", 2, d, KB)
        for m in range(4 if h < HN - 1 else 0):
            add("proj", h + 1, m)
    for d in range(0, KD, 2):
        add("gate", 0, d)
        add("gate", 0, d + 1)
        add("up", 0, d, 0, ends=False)
        add("up", 0, d + 1, KB)
    return tiles


MIXER = mixer_tiles()
MIXER_A = [sum(k[0] != "up" for k in MIXER[:t + 1]) for t in range(len(MIXER))]
MIXER_D = [sum(k[0] == "up" for k in MIXER[:t + 1]) for t in range(len(MIXER))]
INDEX = {k[:3]: t for t, k in enumerate(MIXER)}
PART = 2
FILL_LRU = 8
FILL = {"sum_k": 9, "k_turned": 3, "inv0_turned": 6, "rms_sums": 2}
FILL |= {f"p{s}": 2 for s in range(1, LEVELS)} | {f"qt{s}": 1 for s in range(1, LEVELS)}
FILL |= {"w": 1, "v1": 1, "v2": 1, "v3": 1}

PARTS = [(KB if k[0] == "up" else KD) // PART for k in MIXER]
PARTS_TO = [sum(PARTS[:t + 1]) for t in range(len(MIXER))]
FILL_END = PARTS_TO[INDEX["gate", 0, 1]]


def filled_before(h, step):
    at = FILL_ORDER.index(step)
    return min(FILL_END, 4 * PARTS[0] + FILL_LRU + h * sum(FILL.values()) + sum(FILL.get(s, 0) for s in FILL_ORDER[:at + 1]))


OWNER = {"ffn_up0": "d", "ffn_down0": "d", "att_qk": "a", "att_v": "a", "lru_x": "a", "lru_g": "a", "mixer": "both",
         "mix_out": "d", "mem_k": "a", "mem_v": "a", "x_q": "a", "x_out": "d",
         "ffn_up1": "d", "ffn_down1": "d"}
FREE_D, FREE_A = {}, {}
_d = _a = 0
for _name, _tiles, _units in PHASES:
    FREE_D[_name], FREE_A[_name] = _d, _a
    _d += {"d": _tiles, "a": 0, "both": MIXER_D[-1]}[OWNER[_name]]
    _a += {"a": _tiles, "d": 0, "both": MIXER_A[-1]}[OWNER[_name]]
FREED_D, FREED_A = _d, _a

P_LNG, P_LNB = 0, 4 * KD
P_CW = P_LNB + 4 * KD
P_LCW = P_CW + HN * 12
P_LCB = P_LCW + KB * 4
P_GB = P_LCB + KB
P_LAM = P_GB + 2 * KB
P_NW = P_LAM + KB
P_ALOG = P_NW + 1
P_DT = P_ALOG + 1
PAR = P_DT + 1

C_ID, C_CAUSAL, C_FLIP, C_LEVEL = 0, P, 2 * P, 3 * P
CONST = (3 + LEVELS) * P


class Signal:

    def __init__(self, handle, per_layer, start=0):
        self.sem, self.per_layer, self.start = handle, per_layer, start

    def at(self, layer, n):
        return layer * self.per_layer + (self.start + n)


class StepSignal:

    def __init__(self, handle, steps, rounds):
        self.sem, self.steps, self.rounds, self.next = handle, steps, rounds, 0

    def after(self, layer, rnd, step):
        n = len(self.steps)
        return layer * (n * self.rounds) + rnd * n + (self.steps.index(step) + 1)

    def done(self, ins, step):
        assert self.steps[self.next % len(self.steps)] == step, (step, self.steps[self.next % len(self.steps)])
        self.next += 1
        return ins.then_inc(self.sem, 1)


class Chain:

    def __init__(self, eng, handle):
        self.eng, self.sem, self.base, self.n = eng, handle, 0, 0

    def link(self, ins):
        self.n += 1
        ins.then_inc(self.sem, 1)
        self.eng.wait_ge(self.sem, self.base + self.n)

    @contextmanager
    def loop(self, count, links):
        with self.eng.Fori(0, count) as i:
            base, n = self.base, self.n
            self.base = base + i * links
            yield i
            assert self.n - n == links, f"{self.n - n} links in the loop's body, not {links}"
            self.base, self.n = base, n + count * links


DN_PE = (["sum_k", "sum_q", "decay_rows", "k_turned", "v_turned", "a01", "a23", "inv0_turned"]
         + [f"{x}{s}" for s in range(1, LEVELS) for x in (("p", "qt", "q") if s < LEVELS - 1 else ("p", "qt"))]
         + ["w"] + [f"{x}{c}" for c in range(CH) for x in (("v", "o", "s") if c < CH - 1 else ("v", "o"))]
         + ["rms_sums"])
FILL_ORDER = DN_PE
DN_ACT = (["th1", "th0", "th2", "sq_k", "sq_q", "std_k", "std_q", "exp_g", "decay_exp", "kd_exp", "last_exp", "kg", "vk",
           "inv0"] + [f"p{s}" for s in range(1, LEVELS)] + ["w", "o", "o_sq", "rms_std", "z_th", "y_hi"])
DN_DVE = (["conv1", "conv0", "conv2", "silu1", "silu0", "silu2", "g_row", "k_normed", "q_normed",
           "g_last", "decay_min", "kd_arg", "decay", "kd", "m", "qk", "c0", "t0", "q_dec"]
          + [f"{x}{s}" for s in range(1, LEVELS) for x in (("c", "t", "n") if s < LEVELS - 1 else ("c", "t"))]
          + [f"{x}{c}" for c in range(CH) for x in (("v", "s") if c < CH - 1 else ("v",))]
          + ["o_normed", "z_gate", "y", "y_lo"])
LRU_BESIDE_DVE = ({4 * p + 5 + n: ("conv", p, n) for p in range(KB) for n in range(4)}
                  | {4 * p + 21 + n: ("g_arg", p, n) for p in range(KB) for n in range(2)}
                  | {4 * p + 24: ("g_gate", p, 0) for p in range(KB)})
LRU_BESIDE_ACT = {4 * p + 4: ("x", p) for p in range(KB)} | {4 * p + 20: ("g_sq", p) for p in range(KB)} | {
    4 * p + 23: ("g_th", p) for p in range(KB)}
LRU_BESIDE_END = 4 * (KB - 1) + 25
LRU_ACT = ([f"{x}{p}" for p in range(KB) for x in ("g_sq", "g_th")]
           + [f"{x}{p}" for p in range(KB) for x in ("r", "i", "a", "s")]
           + [f"q{p}" for p in range(KB)] + [f"y_hi{p}" for p in range(KB)])
LRU_DVE = ([f"conv{p}" for p in range(KB)] + [f"{x}{p}" for p in range(KB) for x in ("g_arg", "g_gate")]
           + [f"{x}{p}" for p in range(KB) for x in ("q", "xi")]
           + [x for p in range(KB) for x in ([f"h{p}", f"y{p}"] + ([f"y_lo{p - 1}"] if p else []))] + [f"y_lo{KB - 1}"])



def trunk(nc, xT, memT, stream, par_d, ba_w_d, gate_w_d, table_d, const_d, ext_d, outT):
    with ExitStack() as ctx:
        def sem(name):
            return ctx.enter_context(nc.semaphore(name))

        def sb(name, shape, dt=F32, scope=ctx):
            return scope.enter_context(nc.sbuf_tensor(name, shape, dt))

        xf = sb("xf", [P, KD, SEQ])
        xh = sb("xh", [P, KD, SEQ], F32R)
        xl = sb("xl", [P, KD, SEQ], F32R)
        raw = sb("raw", [P, SLOTS, UNIT])
        wh = sb("wh", [P, SLOTS, UNIT], F32R)
        wl = sb("wl", [P, SLOTS, UNIT], F32R)
        const = sb("const", [P, CONST])
        par = sb("par", [P, PAR])
        tmp = [sb(f"tmp{n}", [P, SEQ]) for n in range(4)]
        y_sum = sb("y_sum", [P, SEQ])
        sq_sum = sb("sq_sum", [P, SEQ])
        ones = sb("ones", [P, P])
        mean_w = sb("mean_w", [P, P])
        eps_rms = sb("eps_rms", [P, 1])
        eps_l2 = sb("eps_l2", [P, 1])
        eps_0 = sb("eps_0", [P, 1])
        warm = sb("warm", [P, 1])

        with ExitStack() as ffn:
            hh = sb("hh", [P, KF, SEQ], F32R, ffn)
            hl = sb("hl", [P, KF, SEQ], F32R, ffn)
        with ExitStack() as mix:
            ych = sb("ych", [P, 2 * KB, SEQ], F32R, mix)
            ycl = sb("ycl", [P, 2 * KB, SEQ], F32R, mix)
            rows = sb("rows", [P, SEQ], F32, mix)
            cols = sb("cols", [P, 3, CH, HN], F32, mix)
            hc = sb("hc", [P, 2, CH], F32, mix)
            lam = sb("lam", [P, 8, KB], F32, mix)
            nea = sb("nea", [32, 2], F32, mix)
            with ExitStack() as att:
                aq = sb("aq", [P, KB, SEQ], F32, att)
                ak = sb("ak", [P, KB, SEQ], F32, att)
                av = sb("av", [P, CH, BRW], F32, att)
                bias = sb("bias", [P, HA, 2 * P], F32, att)
                ext = sb("ext", [HA, 3 * P - 1], F32, att)
                sc = sb("sc", [P, CH, SEQ], F32, att)
                pt = sb("pt", [P, CH, SEQ], F32, att)
                neg_max = sb("neg_max", [P, HA * CH], F32, att)
                row_sum = sb("row_sum", [P, HA * CH], F32, att)
                inv_sum = sb("inv_sum", [P, HA * CH], F32, att)
                lc = sb("lc", [P, KB, SEQ], F32, att)
            gt = sb("gt", [P, 2, SEQ], F32, mix)
            with ExitStack() as lru:
                lr = sb("lr", [P, KB, SEQ], F32, lru)
                li = sb("li", [P, KB, SEQ], F32, lru)
                gate_w = sb("gate_w", [P, 2, KB, P], F32, lru)
            with ExitStack() as dn:
                yah = sb("yah", [P, KB, SEQ], F32R, dn)
                yal = sb("yal", [P, KB, SEQ], F32R, dn)
                with ExitStack() as heads:
                    dt_ = sb("decay", [P, CH, P], F32, heads)
                    mt = sb("mt", [P, CH, P], F32, heads)
                    qk = sb("qk", [P, CH, P], F32, heads)
                    kg = sb("kg", [P, CH, P], F32, heads)
                    kd = sb("kd", [P, CH, P], F32, heads)
                    vk = sb("vk", [P, CH, P], F32, heads)
                    dx = sb("dx", [P, 3, SEQ], F32, heads)
                    dz = sb("dz", [P, 2, SEQ], F32, heads)
                    dc = sb("dc", [P, 3, SEQ], F32, heads)
                    eg = sb("eg", [P, SEQ], F32, heads)
                    state = sb("state", [P, P], F32, heads)
                    vn = sb("vn", [P, P], F32, heads)
                with ExitStack() as mrg:
                    mh = sb("mh", [P, KD, SEQ], F32R, mrg)
                    ml = sb("ml", [P, KD, SEQ], F32R, mrg)
        with ExitStack() as xa:
            xq = sb("xq", [P, KD, SEQ], F32, xa)
            oh = sb("oh", [P, KD, SEQ], F32R, xa)
            ol = sb("ol", [P, KD, SEQ], F32R, xa)
            mraw = sb("mraw", [P, KD, MEM], F32, xa)
            meh = sb("meh", [P, KD, MEM], F32R, xa)
            mel = sb("mel", [P, KD, MEM], F32R, xa)
            xk = sb("xk", [P, KD, MEM], F32, xa)
            x_negmax = sb("x_negmax", [P, HX * CH], F32, xa)
            x_sum = sb("x_sum", [P, HX * CH], F32, xa)
            x_inv = sb("x_inv", [P, HX * CH], F32, xa)
        xv = mraw[:, :, :].rearrange("p k m -> p (k m)").rearrange("p (a f) -> p a f", a=KM)

        lx, lg = xf[:, 0:KB, :], xf[:, KB:2 * KB, :]
        ba_w = sc[:, 0, :].rearrange("p (k m) -> p k m", k=KD)
        row_f = pt[0:HN, 0, :]
        os_, tt = eg, dt_

        ident = const[:, C_ID:C_ID + P]
        flip = const[:, C_FLIP:C_FLIP + P]
        causal = const[:, C_CAUSAL:C_CAUSAL + P]

        def level_mask(s):
            m = const[:, C_LEVEL + s * P:C_LEVEL + (s + 1) * P]
            return m.rearrange("p (a b) -> p a b", a=1).broadcast_to([P, CH, P])

        x_loaded, const_loaded, par_loaded = sem("x_loaded"), sem("const_loaded"), sem("par_loaded")
        mix_par_loaded = [sem(f"mix_par_loaded{n}") for n in range(3)]
        ext_stored, bias_loaded, mem_loaded, out_stored = sem("ext_stored"), sem("bias_loaded"), sem("mem_loaded"), sem("out_stored")
        unit_loaded = [sem(f"unit_loaded{s}") for s in range(SLOTS)]
        hi_step, unit_split, unit_begun = sem("hi_step"), sem("unit_split"), sem("unit_begun")
        consts_set, waited_apart = sem("consts_set"), sem("waited_apart")
        acc_ready = Signal(sem("acc_ready"), TILES)
        freed_d = Signal(sem("freed_d"), FREED_D, start=4)
        freed_a = Signal(sem("freed_a"), FREED_A, start=4)
        silu_th = Signal(sem("silu_th"), 2 * KF)
        inner_hi = Signal(sem("inner_hi"), 2 * KF)
        inner_lo = Signal(sem("inner_lo"), 2 * KF)
        y_sq = Signal(sem("y_sq"), 4 * KD)
        y_added, sq_added = (Signal(sem(n), 4 * KD, start=1) for n in ("y_added", "sq_added"))
        sums_ready, x_whole = Signal(sem("sums_ready"), 4), Signal(sem("x_whole"), KD)
        variance, deviation = Signal(sem("variance"), 4), Signal(sem("deviation"), 4)
        centred, affine = Signal(sem("centred"), 4 * KD), Signal(sem("affine"), 4 * KD)
        x_hi, x_lo = Signal(sem("x_hi"), 4 * KD, KD), Signal(sem("x_lo"), 4 * KD, KD)
        ext_padded = Signal(sem("ext_padded"), 1)
        bias_flipped, bias_copied = Signal(sem("bias_flipped"), 4), Signal(sem("bias_copied"), 4)
        bias_masked = Signal(sem("bias_masked"), 1)
        scores = Signal(sem("scores"), HA * CH)
        biased, row_max = Signal(sem("biased"), HA * CH), Signal(sem("row_max"), HA * CH)
        exps, probs = Signal(sem("exps"), HA * CH), Signal(sem("probs"), HA * CH)
        turned, turned_out = Signal(sem("turned"), HA * CH), Signal(sem("turned_out"), HA * CH)
        att_out = Signal(sem("att_out"), HA, start=1)
        yc_hi, yc_lo = Signal(sem("yc_hi"), KB), Signal(sem("yc_lo"), KB)
        lru_act, lru_dve = StepSignal(sem("lru_act"), LRU_ACT, 1), StepSignal(sem("lru_dve"), LRU_DVE, 1)
        lru_gates = Signal(sem("lru_gates"), 2 * KB)
        lam_arg, lam_exp, lam_ready = (Signal(sem(n), 1) for n in ("lam_arg", "lam_exp", "lam_ready"))
        ba_ready, rows_turned = Signal(sem("ba_ready"), 1), Signal(sem("rows_turned"), 1)
        row_arg, row_exp, rows_ready, cols_ready = (Signal(sem(n), 1) for n in ("row_arg", "row_exp", "rows_ready", "cols_ready"))
        beta_th, cols_exp = Signal(sem("beta_th"), 1), Signal(sem("cols_exp"), 1)
        dn_pe, dn_act, dn_dve = (StepSignal(sem(n), steps, HN) for n, steps in (("dn_pe", DN_PE), ("dn_act", DN_ACT), ("dn_dve", DN_DVE)))
        partial = Signal(sem("partial"), KD)
        merged, merged_hi, merged_lo = (Signal(sem(n), KD) for n in ("merged", "merged_hi", "merged_lo"))
        mem_hi, mem_lo = Signal(sem("mem_hi"), 1), Signal(sem("mem_lo"), 1)
        x_scores, x_row_max, x_exps, x_probs, x_turned, x_turned_out = (
            Signal(sem(n), HX * CH) for n in ("x_scores", "x_row_max", "x_exps", "x_probs", "x_turned", "x_turned_out"))
        x_att_out = Signal(sem("x_att_out"), 2 * HX, start=1)
        xo_hi, xo_lo = (Signal(sem(n), 2 * HX) for n in ("xo_hi", "xo_lo"))
        dve_step, act_step = sem("dve_step"), sem("act_step")

        acc = ctx.enter_context(nc.psum_tensor("acc", [P, 4, SEQ], F32))
        aux = ctx.enter_context(nc.psum_tensor("aux", [P, 4, SEQ], F32))
        B4, B5, B6, B7 = (aux[:, n, :] for n in range(4))

        def x_sc(n):
            return tmp[(n % 4) // 2][:, (n % 2) * MEM:(n % 2 + 1) * MEM]

        def tiles(bank):
            bank = bank[:, :]
            return bank.rearrange("p (c m) -> p c m", c=CH)

        def wait_apart(eng, sem_, value):
            eng.wait_ge(sem_, value)
            eng.sem_inc(waited_apart, 1)

        ROUNDS = DEPTH * UNITS // SLOTS
        block = ctx.enter_context(nc.Block())

        @block.sync
        def _(sp):
            sp.dma_start(xf[:, :, :], xT.rearrange("(k p) t -> p k t", p=P)).then_inc(x_loaded, 16)
            for s in range(SLOTS):
                sp.dma_start(raw[:, s, :], stream[s]).then_inc(unit_loaded[s], 16)
            with sp.Fori(1, ROUNDS) as i:
                for s in range(SLOTS):
                    sp.wait_ge(unit_split, i * SLOTS + (s - SLOTS + 1))
                    sp.dma_start(raw[:, s, :], stream[i * SLOTS + s]).then_inc(unit_loaded[s], 16)
            sp.wait_ge(x_hi.sem, x_hi.start + DEPTH * x_hi.per_layer)
            sp.dma_start(outT.rearrange("(k p) t -> p k t", p=P), xf[:, :, :]).then_inc(out_stored, 16)
            sp.wait_ge(out_stored, 16)

        @block.gpsimd
        def _(pool):
            pool.dma_start(const[:, :], const_d).then_inc(const_loaded, 16)
            pool.memset(ones[:, :], 1.0).then_inc(consts_set, 1)
            pool.memset(mean_w[:, :], 1.0 / DM).then_inc(consts_set, 1)
            pool.memset(eps_rms[:, :], NORM_EPS).then_inc(consts_set, 1)
            pool.memset(eps_l2[:, :], 4 * NORM_EPS).then_inc(consts_set, 1)
            pool.memset(eps_0[:, :], 0.0).then_inc(consts_set, 1)

            def split(i, s):
                pool.tensor_scalar(wh[:, s, :], raw[:, s, :], 1.0, 0.0, ALU.mult, ALU.add).then_inc(hi_step, 1)
                pool.wait_ge(hi_step, i * SLOTS + (s + 1))
                pool.tensor_tensor(wl[:, s, :], raw[:, s, :], wh[:, s, :].bitcast(F32), ALU.subtract).then_inc(unit_split, 1)

            for s in range(SLOTS):
                pool.wait_ge(unit_loaded[s], 16)
                split(0, s)
            with pool.Fori(1, ROUNDS) as i:
                for s in range(SLOTS):
                    pool.wait_ge(unit_loaded[s], i * 16 + 16)
                    wait_apart(pool, unit_begun, i * SLOTS + (s - SLOTS + 2))
                    split(i, s)

        @block.tensor
        def _(pe):
            def mm(out, w, x, start=True, stop=True):
                return pe.matmul(out, w, x, start=start, stop=stop, skip_group_check=True)

            def three(out, w_hi, w_lo, x_hi_, x_lo_, start, stop, begins=False):
                first = mm(out, w_hi, x_hi_, start, False)
                if begins:
                    first.then_inc(unit_begun, 1)
                mm(out, w_hi, x_lo_, False, False)
                return mm(out, w_lo, x_hi_, False, stop)

            def unit_here(layer, u):
                pe.wait_ge(unit_split, layer * UNITS + (u + 1))

            def unit(out, s, k_tiles, at, rhs, start, stop, ready=None, begins=True):
                for n, k in enumerate(k_tiles):
                    if ready is not None:
                        ready(k)
                    c = slice((at + n) * P, (at + n + 1) * P)
                    last = three(out, wh[:, s, c], wl[:, s, c], *rhs(k), start and n == 0,
                                 stop and n == len(k_tiles) - 1, begins=begins and n == 0)
                return last

            def of_x(k):
                return xh[:, k, :], xl[:, k, :]

            def x_ready(l, norm):
                return lambda k: pe.wait_ge(x_lo.sem, x_lo.at(l, (norm - 1) * KD + k + 1))

            def free_bank(l, name, t):
                sig, base = (freed_d, FREE_D[name]) if OWNER[name] == "d" else (freed_a, FREE_A[name])
                pe.wait_ge(sig.sem, sig.at(l, base) + t)

            def simple_tile(l, name, n, ready=None, cols=slice(0, SEQ), rhs=of_x, i=0):
                free_bank(l, name, i * 4 + (n - 3))
                unit_here(l, i * 4 + (UNIT0[name] + n))
                unit(acc[:, n % 4, cols], n % SLOTS, range(KD), 0, rhs, True, True, ready).then_inc(acc_ready.sem, 1)

            def first_four(l, name, norm):
                free_bank(l, name, 0)
                ready = x_ready(l, norm)
                for k in range(KD):
                    ready(k)
                    for n in range(4):
                        if k == 0:
                            unit_here(l, UNIT0[name] + n)
                        c = slice(k * P, (k + 1) * P)
                        last = three(acc[:, n, :], wh[:, n, c], wl[:, n, c], *of_x(k), k == 0, k == KD - 1,
                                     begins=k == (KD - 1 if n else 0))
                        if k == KD - 1:
                            last.then_inc(acc_ready.sem, 1)

            def out_projection(l, name, norm, tile):
                with pe.Fori(0, KD // 4) as i:
                    for n in range(4):
                        free_bank(l, name, i * 4 + (n - 3))
                        tile(i, n).then_inc(acc_ready.sem, 1)
                pe.wait_ge(y_added.sem, y_added.at(l, (norm + 1) * KD))
                mm(B4, mean_w[:, :], y_sum[:, :])
                pe.wait_ge(sq_added.sem, sq_added.at(l, (norm + 1) * KD))
                mm(B5, mean_w[:, :], sq_sum[:, :]).then_inc(sums_ready.sem, 1)

            def one_unit(l, name, rhs, ready):
                def tile(i, n):
                    unit_here(l, i * 4 + (UNIT0[name] + n))
                    return unit(acc[:, n, :], n, range(KD), 0, rhs, True, True, ready if n == 0 else None)
                return tile

            def ffn(l, which, norm):
                up, down = f"ffn_up{which}", f"ffn_down{which}"
                first_four(l, up, norm)
                with pe.Fori(1, KF // 2) as i:
                    for n in range(4):
                        simple_tile(l, up, n, i=i)

                def inner_ready(k):
                    pe.wait_ge(inner_lo.sem, inner_lo.at(l, which * KF + k + 1))

                def tile(i, n):
                    parts = [range(0, 8), range(8, 16), range(16, KF)]
                    for m, ks in enumerate(parts):
                        unit_here(l, i * 12 + (UNIT0[down] + 3 * n + m))
                        last = unit(acc[:, n, :], (3 * n + m) % SLOTS, ks, 0, lambda k: (hh[:, k, :], hl[:, k, :]),
                                    m == 0, m == 2, inner_ready if n == 0 else None)
                    return last
                out_projection(l, down, norm, tile)

            def attention(l):
                first_four(l, "att_qk", 1)
                ba_product(l)
                for n in range(KB, 2 * KB):
                    simple_tile(l, "att_qk", n)
                for t in range(CH):
                    free_bank(l, "att_v", t - 3)
                for n in range(4):
                    unit_here(l, UNIT0["att_v"] + n)
                    for t in range(CH):
                        for m in range(2):
                            k, c = 2 * n + m, slice(m * BRW, (m + 1) * BRW)
                            tok = slice(t * P, (t + 1) * P)
                            o = acc[:, t, :]
                            first = mm(o, xh[:, k, tok], wh[:, n, c], k == 0, False)
                            if t == 0 and m == 0:
                                first.then_inc(unit_begun, 1)
                            mm(o, xh[:, k, tok], wl[:, n, c], False, False)
                            last = mm(o, xl[:, k, tok], wh[:, n, c], False, k == KD - 1)
                        if n == 3:
                            last.then_inc(acc_ready.sem, 1)

                pe.wait_ge(rows_ready.sem, rows_ready.at(l, 1))
                for c in range(CH):
                    last = pe.transpose(tiles(B6)[:, c, :], rows[:, c * P:(c + 1) * P], ident)
                last.then_inc(rows_turned.sem, 1)
                pe.wait_ge(cols_ready.sem, cols_ready.at(l, 1))
                pe.wait_ge(freed_a.sem, freed_a.at(l, FREE_A["att_v"] + CH))

                pe.wait_ge(bias_loaded, l * 16 + 16)
                for m in range(4):
                    mm(aux[:, m, :], flip, bias[:, 2 * m:2 * m + 2, :]).then_inc(bias_flipped.sem, 1)
                pe.wait_ge(bias_copied.sem, bias_copied.at(l, 4))

                def score(n):
                    h, i = divmod(n, CH)
                    rows_ = slice(HDA * (h % 2), HDA * (h % 2) + HDA)
                    if n >= 2:
                        pe.wait_ge(biased.sem, biased.at(l, n - 1))
                    mm(aux[:, n % 2, 0:(i + 1) * P], aq[rows_, h // 2, i * P:(i + 1) * P],
                       ak[rows_, h // 2, 0:(i + 1) * P]).then_inc(scores.sem, 1)

                def turn(n):
                    h, i = divmod(n, CH)
                    pe.wait_ge(probs.sem, probs.at(l, n + 1))
                    if n >= 2:
                        pe.wait_ge(turned_out.sem, turned_out.at(l, n - 1))
                    for j in range(i + 1):
                        last = pe.transpose(aux[:, 2 + n % 2, j * P:(j + 1) * P], sc[:, i, j * P:(j + 1) * P], ident)
                    last.then_inc(turned.sem, 1)

                def values(h):
                    bank = acc[HDA * (h % 2):HDA * (h % 2) + HDA, (h // 2) % 2, :]
                    pe.wait_ge(turned_out.sem, turned_out.at(l, CH * (h + 1)))
                    if h % 2 == 0 and h >= 4:
                        pe.wait_ge(yc_lo.sem, yc_lo.at(l, h // 2 - 1))
                    for j in range(CH):
                        last = mm(bank[:, j * P:SEQ], av[:, j, h * HDA:(h + 1) * HDA], pt[:, j, j * P:SEQ],
                                  j == 0, j == CH - 1)
                    last.then_inc(att_out.sem, 1)

                def lru_part(n):
                    j, part = divmod(n, CH)
                    o = acc[:, 2 + j % 2, :]
                    if part == 0:
                        unit_here(l, UNIT0["lru_x"] + j)
                        if j >= 2:
                            pe.wait_ge(freed_a.sem, freed_a.at(l, FREE_A["lru_x"] + j - 1))
                    k = part * (KD // CH)
                    last = unit(o, j % SLOTS, range(k, k + KD // CH), k, of_x, part == 0, part == CH - 1,
                                begins=part == 0)
                    if part == CH - 1:
                        last.then_inc(acc_ready.sem, 1)

                score(0)
                score(1)
                for n in range(HA * CH):
                    lru_part(n)
                    turn(n)
                    if n + 2 < HA * CH:
                        score(n + 2)
                    if n % CH == CH - 1:
                        values(n // CH)
                pe.wait_ge(yc_lo.sem, yc_lo.at(l, KB))

            def rg_lru(l):
                for p in range(KB):
                    fill(l, PARTS[0])
                    if p == 0:
                        pe.wait_ge(lru_dve.sem, lru_dve.after(l, 0, f"conv{KB - 1}"))
                        pe.wait_ge(mix_par_loaded[0], l * 16 + 16)
                    if p >= 2:
                        pe.wait_ge(lru_act.sem, lru_act.after(l, 0, f"i{p - 2}"))
                    for g in range(2):
                        mm(aux[:, 2 * (p % 2) + g, :], gate_w[:, g, p, :], lc[:, p, :]).then_inc(lru_gates.sem, 1)
                fill(l, FILL_LRU)
                pe.wait_ge(lru_act.sem, lru_act.after(l, 0, "i3"))

            def ba_product(l):
                pe.wait_ge(mix_par_loaded[1], l * 16 + 16)
                for k in range(KD):
                    last = mm(B7[0:64, :], ba_w[:, k, :], xf[:, k, :], k == 0, k == KD - 1)
                last.then_inc(ba_ready.sem, 1)

            mixer = [(t, part) for t in range(len(MIXER)) for part in range(PARTS[t])]
            mixer_at = [0]

            def fill(l, parts, branch_a=False):
                for _ in range(parts):
                    if mixer_at[0] == len(mixer):
                        return
                    t, part = mixer[mixer_at[0]]
                    kind, a, b, u, at = MIXER[t]
                    if (kind, a) == ("up", 0) and not branch_a:
                        return
                    mixer_at[0] += 1
                    if part == 0:
                        if t < 4:
                            free_bank(l, "mixer", t - 3)
                        elif MIXER[t - 4][0] == "up":
                            pe.wait_ge(freed_d.sem, freed_d.at(l, FREE_D["mixer"] + MIXER_D[t - 4]))
                        else:
                            pe.wait_ge(freed_a.sem, freed_a.at(l, FREE_A["mixer"] + MIXER_A[t - 4]))
                        if at == 0:
                            unit_here(l, UNIT0["mixer"] + u)
                    o = acc[:, t % 4, :]
                    if (kind, a, b, part) == ("up", 1, 0, 0):
                        pe.wait_ge(lru_dve.sem, lru_dve.after(l, 0, "y_lo3"))
                    at += part * PART
                    k = (KB * a if kind == "up" else 0) + part * PART
                    last = unit(o, u % SLOTS, range(k, k + PART), at, of_y if kind == "up" else of_x, part == 0,
                                part == PARTS[t] - 1, begins=at == 0)
                    if part == PARTS[t] - 1:
                        last.then_inc(acc_ready.sem, 1)

            def delta(l):
                for h in range(HN):
                    def dve(step):
                        pe.wait_ge(dn_dve.sem, dn_dve.after(l, h, step))

                    def act(step):
                        pe.wait_ge(dn_act.sem, dn_act.after(l, h, step))

                    done = dn_pe.done

                    fill(l, FILL["sum_k"])
                    act("sq_k")
                    done(mm(B7, ones[:, :], tmp[1][:, :]), "sum_k")
                    act("sq_q")
                    done(mm(B6, ones[:, :], tmp[0][:, :]), "sum_q")
                    dve("g_row")
                    done(mm(B5, ones[0:HN, :], mt[0:HN, :, :]), "decay_rows")
                    fill(l, FILL["k_turned"])
                    dve("k_normed")
                    for c in range(CH):
                        last = pe.transpose(tiles(B4)[:, c, :], dc[:, 1, c * P:(c + 1) * P], ident)
                    done(last, "k_turned")
                    act("std_q")
                    for c in range(CH):
                        last = pe.transpose(tiles(B6)[:, c, :], dc[:, 2, c * P:(c + 1) * P], ident)
                    done(last, "v_turned")
                    dve("q_normed")
                    for m, bank in enumerate((B7, B5)):
                        if m == 1:
                            act("exp_g")
                            dve("decay_min")
                        for n in range(2):
                            c = 2 * m + n
                            tok = slice(c * P, (c + 1) * P)
                            for part in (1, 0):
                                o = tiles(bank)[:, 2 * n + (1 - part), :]
                                last = mm(o, dc[:, 1, tok], dc[:, part, tok])
                        done(last, ("a01", "a23")[m])
                    fill(l, FILL["inv0_turned"])
                    dve("t0")
                    act("kg")
                    dve("kd")
                    for c in range(CH):
                        last = pe.transpose(tiles(B4)[:, c, :], tt[:, c, :], ident)
                    done(last, "inv0_turned")
                    for s in range(1, LEVELS):
                        fill(l, FILL[f"p{s}"])
                        dve(f"c{s}")
                        act("inv0" if s == 1 else f"p{s - 1}")
                        if s > 1:
                            dve(f"n{s - 1}")
                        for c in range(CH):
                            last = mm(tiles(B4)[:, c, :], tiles(tmp[1])[:, c, :], tiles(tmp[0])[:, c, :])
                        done(last, f"p{s}")
                        fill(l, FILL[f"qt{s}"])
                        act(f"p{s}")
                        if s == 1:
                            act("vk")
                            dve("qk")
                        for c in range(CH):
                            last = mm(tiles(B6)[:, c, :], tiles(tmp[2])[:, c, :], tt[:, c, :])
                        done(last, f"qt{s}")
                        if s < LEVELS - 1:
                            for c in range(CH):
                                last = mm(tiles(B7)[:, c, :], tt[:, c, :], tiles(tmp[2])[:, c, :])
                            done(last, f"q{s}")
                    fill(l, FILL["w"])
                    dve(f"t{LEVELS - 1}")
                    for c in range(CH):
                        last = mm(tiles(B4)[:, c, :], kg[:, c, :], tt[:, c, :])
                    done(last, "w")
                    act("w")
                    dve("q_dec")
                    for c in range(CH):
                        fill(l, FILL.get(f"v{c}", 0))
                        if c:
                            dve(f"s{c - 1}")
                        o = B6[:, 0:P]
                        last = mm(o, tt[:, c, :], vk[:, c, :], True, c == 0)
                        if c:
                            last = mm(o, tiles(tmp[2])[:, c, :], state[:, :], False, True)
                        done(last, f"v{c}")
                        dve(f"v{c}")
                        o = tiles(B5)[:, c, :]
                        if c:
                            mm(o, state[:, :], dc[:, 0, c * P:(c + 1) * P], True, False)
                        done(mm(o, vn[:, :], qk[:, c, :], c == 0, True), f"o{c}")
                        if c < CH - 1:
                            done(mm(B7[:, 0:P], kd[:, c, :], vn[:, :]), f"s{c}")
                    fill(l, FILL["rms_sums"])
                    act("o_sq")
                    done(mm(B4, ones[:, :], tmp[3][:, :]), "rms_sums")

            def merge(l):
                fill(l, 2 * PARTS[0])
                wait_apart(pe, dn_dve.sem, dn_dve.after(l, HN - 1, "y_lo"))
                fill(l, len(mixer), branch_a=True)
                assert mixer_at[0] == len(mixer)

            def of_y(k):
                if k < KB:
                    return yah[:, k, :], yal[:, k, :]
                return ych[:, k - KB, :], ycl[:, k - KB, :]

            def memory_kv(l):
                pe.wait_ge(freed_d.sem, freed_d.at(l, FREE_D["mix_out"] + KD))
                pe.wait_ge(mem_lo.sem, mem_lo.at(l, 1))
                for n in range(KD):
                    simple_tile(l, "mem_k", n, cols=slice(0, MEM), rhs=lambda k: (meh[:, k, :], mel[:, k, :]))
                for t in range(4):
                    free_bank(l, "mem_v", t - 3)
                for k in range(KD):
                    unit_here(l, UNIT0["mem_v"] + k)
                    for t in range(4):
                        tok = slice((t // 2) * P, (t // 2 + 1) * P)
                        c = slice((t % 2) * SEQ, (t % 2 + 1) * SEQ)
                        s = k % SLOTS
                        first = mm(acc[:, t, :], meh[:, k, tok], wh[:, s, c], k == 0, False)
                        if t == 0:
                            first.then_inc(unit_begun, 1)
                        mm(acc[:, t, :], meh[:, k, tok], wl[:, s, c], False, False)
                        last = mm(acc[:, t, :], mel[:, k, tok], wh[:, s, c], False, k == KD - 1)
                        if k == KD - 1:
                            last.then_inc(acc_ready.sem, 1)

            def cross_attention(l):
                first_four(l, "x_q", 2)
                for n in range(4):
                    simple_tile(l, "x_q", n, i=1)
                pe.wait_ge(freed_a.sem, freed_a.at(l, FREE_A["x_q"] + KD))

                def score(n):
                    h, i = divmod(n, CH)
                    if n >= 2:
                        pe.wait_ge(x_exps.sem, x_exps.at(l, n - 1))
                    for m in range(2):
                        last = mm(aux[:, n % 2, 0:MEM], xq[:, 2 * h + m, i * P:(i + 1) * P], xk[:, 2 * h + m, :], m == 0, m == 1)
                    last.then_inc(x_scores.sem, 1)

                def turn(n):
                    pe.wait_ge(x_probs.sem, x_probs.at(l, n + 1))
                    if n >= 2:
                        pe.wait_ge(x_turned_out.sem, x_turned_out.at(l, n - 1))
                    for j in range(KM):
                        last = pe.transpose(aux[:, 2 + n % 2, j * P:(j + 1) * P], x_sc(n)[:, j * P:(j + 1) * P], ident)
                    last.then_inc(x_turned.sem, 1)

                def values(h):
                    pe.wait_ge(x_turned_out.sem, x_turned_out.at(l, CH * (h + 1)))
                    for m in range(2):
                        if h:
                            pe.wait_ge(xo_lo.sem, xo_lo.at(l, 2 * h + m - 1))
                        for j in range(KM):
                            f = slice((2 * h + m) * P, (2 * h + m + 1) * P)
                            last = mm(acc[:, 2 + m, :], xv[:, j, f], tmp[2 + j][:, :], j == 0, j == KM - 1)
                        last.then_inc(x_att_out.sem, 1)

                score(0)
                score(1)
                for n in range(HX * CH):
                    turn(n)
                    if n + 2 < HX * CH:
                        score(n + 2)
                    if n % CH == CH - 1:
                        values(n // CH)

            pe.sem_inc(att_out.sem, 1)
            pe.sem_inc(x_att_out.sem, 1)
            pe.wait_ge(consts_set, 5)
            pe.wait_ge(const_loaded, 16)
            with pe.Fori(0, DEPTH) as l:
                ffn(l, 0, 0)
                attention(l)
                rg_lru(l)
                delta(l)
                merge(l)
                wait_apart(pe, freed_a.sem, freed_a.at(l, FREE_A["mixer"] + MIXER_A[-1]))
                out_projection(l, "mix_out", 1, one_unit(
                    l, "mix_out", lambda k: (mh[:, k, :], ml[:, k, :]),
                    lambda k: pe.wait_ge(merged_lo.sem, merged_lo.at(l, k + 1))))
                memory_kv(l)
                cross_attention(l)
                out_projection(l, "x_out", 2, one_unit(
                    l, "x_out", lambda k: (oh[:, k, :], ol[:, k, :]),
                    lambda k: pe.wait_ge(xo_lo.sem, xo_lo.at(l, k + 1))))
                ffn(l, 1, 3)

        HALF_STEP = 0.5 * 0.5 / ALPHA
        GATE_STEP = 0.5 / ALPHA
        GELU_IN = float(np.sqrt(2.0 / np.pi))

        @block.scalar
        def _(act):
            chain = Chain(act, act_step)

            def fn(out, in_, func, **kw):
                return act.activation(out, in_, func, **kw)

            def tile_ready(l, name, n):
                act.wait_ge(acc_ready.sem, acc_ready.at(l, TILE0[name] + 1) + n)

            def ffn_inner(l, which):
                up = f"ffn_up{which}"
                with act.Fori(0, KF // 2) as i:
                    for m in range(2):
                        tile_ready(l, up, i * 4 + 2 * m)
                        act.wait_ge(freed_d.sem, freed_d.at(l, FREE_D[up] + 2 * m) + i * 4)
                        fn(tmp[0][:, :], acc[:, 2 * m, :], ACT.Tanh, scale=0.5).then_inc(silu_th.sem, 1)
                        act.wait_ge(freed_d.sem, freed_d.at(l, FREE_D[up] + 2 * m + 2) + i * 4)
                        fn(hh[:, i * 2 + m, :], tmp[2][:, :], ACT.Copy).then_inc(inner_hi.sem, 1)

            def out_projection(l, name, norm):
                with act.Fori(0, KD // 4) as i:
                    for n in range(4):
                        d = i * 4 + n
                        act.wait_ge(freed_d.sem, freed_d.at(l, FREE_D[name] + 1) + d)
                        wait_apart(act, sq_added.sem, sq_added.at(l, norm * KD) + d)
                        fn(tmp[3][:, :], xf[:, d, :], ACT.Square).then_inc(y_sq.sem, 1)

            def layer_norm(l, norm):
                act.wait_ge(variance.sem, variance.at(l, norm + 1))
                fn(tmp[0][:, :], tmp[3][:, :], ACT.Sqrt, bias=eps_0[:, :]).then_inc(deviation.sem, 1)
                act.wait_ge(par_loaded, l * 16 + 16)
                for d in range(KD):
                    act.wait_ge(centred.sem, centred.at(l, norm * KD + d + 1))
                    c = norm * KD + d
                    fn(xf[:, d, :], xf[:, d, :], ACT.Identity, scale=par[:, P_LNG + c:P_LNG + c + 1],
                       bias=par[:, P_LNB + c:P_LNB + c + 1]).then_inc(affine.sem, 1)
                    act.wait_ge(affine.sem, affine.at(l, norm * KD + d + 1))
                    fn(xh[:, d, :], xf[:, d, :], ACT.Copy).then_inc(x_hi.sem, 1)

            def attention(l):
                for n in range(2 * KB):
                    tile_ready(l, "att_qk", n)
                    dst, scale = (aq[:, n, :], HDA ** -0.5) if n < KB else (ak[:, n - KB, :], 1.0)
                    fn(dst, acc[:, n % 4, :], ACT.Copy, scale=scale).then_inc(freed_a.sem, 1)
                    if n == KB - 1:
                        delta_rows(l)
                for t in range(CH):
                    tile_ready(l, "att_v", t)
                    fn(av[:, t, :], acc[:, t, :], ACT.Copy).then_inc(freed_a.sem, 1)
                act.wait_ge(lam_arg.sem, lam_arg.at(l, 1))
                fn(lam[:, 2, :], lam[:, 1, :], ACT.Exp, scale=-1.0).then_inc(lam_exp.sem, 1)
                act.wait_ge(cols_ready.sem, cols_ready.at(l, 1))
                fn(cols[:, 2, :, :], cols[:, 0, :, :], ACT.Exp).then_inc(cols_exp.sem, 1)

                def turned_copy(n):
                    h, i = divmod(n, CH)
                    act.wait_ge(turned.sem, turned.at(l, n + 1))
                    act.wait_ge(att_out.sem, att_out.at(l, h))
                    fn(pt[:, 0:i + 1, i * P:(i + 1) * P], tiles(aux[:, 2 + n % 2, :])[:, 0:i + 1, :],
                       ACT.Copy).then_inc(turned_out.sem, 1)

                def out_copy(pair):
                    act.wait_ge(att_out.sem, att_out.at(l, 2 * pair + 2))
                    fn(ych[:, KB + pair, :], acc[:, pair % 2, :], ACT.Copy).then_inc(yc_hi.sem, 1)

                for n in range(HA * CH):
                    i = n % CH
                    act.wait_ge(row_max.sem, row_max.at(l, n + 1))
                    s = sc[:, i, 0:(i + 1) * P]
                    fn(s, s, ACT.Exp, bias=neg_max[:, n:n + 1], accum_out=row_sum[:, n:n + 1]).then_inc(exps.sem, 1)
                    if n >= 1:
                        turned_copy(n - 1)
                    if n >= 2 and (n - 1) % (2 * CH) == 0:
                        out_copy((n - 1) // (2 * CH) - 1)
                    lru_beside(l, n)
                turned_copy(HA * CH - 1)
                out_copy(KB - 1)
                act.dma_start(gate_w[:, :, :, :], gate_w_d[l]).then_inc(mix_par_loaded[0], 16)
                for n in range(HA * CH, LRU_BESIDE_END):
                    lru_beside(l, n)

            def lru_beside(l, n):
                step, p = LRU_BESIDE_ACT.get(n, (None, None))
                if step == "x":
                    tile_ready(l, "lru_x", p)
                    fn(lx[:, p, :], acc[:, 2 + p % 2, :], ACT.Copy).then_inc(freed_a.sem, 1)
                elif step == "g_sq":
                    if p:
                        act.wait_ge(lru_act.sem, lru_act.after(l, 0, f"g_th{p - 1}"))
                    tile_ready(l, "lru_g", p)
                    lru_act.done(fn(tmp[0][:, :], acc[:, 2 + p % 2, :], ACT.Square), f"g_sq{p}")
                    fn(lg[:, p, :], acc[:, 2 + p % 2, :], ACT.Copy).then_inc(freed_a.sem, 1)
                elif step == "g_th":
                    act.wait_ge(lru_dve.sem, lru_dve.after(l, 0, f"g_arg{p}"))
                    lru_act.done(fn(tmp[1][:, :], tmp[0][:, :], ACT.Tanh, scale=GELU_IN), f"g_th{p}")

            def rg_lru(l):
                def dve(step):
                    act.wait_ge(lru_dve.sem, lru_dve.after(l, 0, step))

                def own(step):
                    act.wait_ge(lru_act.sem, lru_act.after(l, 0, step))
                done = lru_act.done
                act.wait_ge(lam_ready.sem, lam_ready.at(l, 1))
                for p in range(KB):
                    mixer_tile(l, p)
                    for g, dst in enumerate((lr, li)):
                        act.wait_ge(lru_gates.sem, lru_gates.at(l, 2 * p + g + 1))
                        done(fn(dst[:, p, :], aux[:, 2 * (p % 2) + g, :], ACT.Tanh, scale=0.5,
                                bias=lam[:, 6 + g, p:p + 1]), f"{'ri'[g]}{p}")
                    own(f"r{p}")
                    done(fn(lx[:, p, :], lr[:, p, :], ACT.Exp, scale=lam[:, 4, p:p + 1], bias=lam[:, 4, p:p + 1]), f"a{p}")
                    done(fn(lr[:, p, :], lr[:, p, :], ACT.Tanh, scale=lam[:, 5, p:p + 1], bias=lam[:, 5, p:p + 1]), f"s{p}")
                for p in range(KB):
                    dve(f"q{p}")
                    done(fn(lr[:, p, :], lr[:, p, :], ACT.Sqrt, scale=0.5, bias=eps_0[:, :]), f"q{p}")
                drain(l, 4 * PARTS[0] + FILL_LRU)
                for p in range(KB):
                    dve(f"y{p}")
                    done(fn(ych[:, p, :], tmp[p % 2][:, :], ACT.Copy), f"y_hi{p}")

            def delta_rows(l):
                act.wait_ge(row_arg.sem, row_arg.at(l, 1))
                fn(tmp[1][0:HN, :], tmp[0][0:HN, :], ACT.Exp, scale=-1.0)
                fn(nea[0:HN, 0:1], par[0:HN, P_ALOG:P_ALOG + 1], ACT.Exp).then_inc(row_exp.sem, 1)
                fn(rows[32:32 + HN, :], B7[32:32 + HN, :], ACT.Tanh, scale=0.5).then_inc(beta_th.sem, 1)

            def mixer_tile(l, t):
                kind, a, b = MIXER[t][:3]
                tile_ready(l, "mixer", t)
                if kind == "proj":
                    if a:
                        act.wait_ge(dn_dve.sem, dn_dve.after(l, a - 1, "conv2"))
                    fn(dx[:, b, :] if b < 3 else dz[:, a % 2, :], acc[:, t % 4, :], ACT.Copy).then_inc(freed_a.sem, 1)
                    return
                slot = a - 1 if a else b % 2
                if a == 2 or (a == 0 and b == 1):
                    if b or a == 0:
                        act.wait_ge(partial.sem, partial.at(l, b if a else KD))
                elif a == 0 and b >= 2:
                    act.wait_ge(merged.sem, merged.at(l, b - 1))
                elif a == 0 or b:
                    act.wait_ge(freed_d.sem, freed_d.at(l, FREE_D["mixer"] + MIXER_D[INDEX["up", 1, b - 1 if a else KD - 1]]))
                fn(gt[:, slot, :], acc[:, t % 4, :], ACT.Tanh, scale=0.5).then_inc(freed_a.sem, 1)

            drained = [KB]

            def drain(l, count):
                while drained[0] < len(MIXER) and PARTS_TO[drained[0]] <= count:
                    if MIXER[drained[0]][0] != "up":
                        mixer_tile(l, drained[0])
                    drained[0] += 1

            def delta(l):
                act.wait_ge(cols_exp.sem, cols_exp.at(l, 1))
                for h in range(HN):
                    def dve(step):
                        act.wait_ge(dn_dve.sem, dn_dve.after(l, h, step))

                    def pe_(step):
                        drain(l, filled_before(h, step))
                        act.wait_ge(dn_pe.sem, dn_pe.after(l, h, step))
                    done = dn_act.done
                    for m in (1, 0, 2):
                        dve(f"conv{m}")
                        done(fn(tmp[m][:, :], dc[:, m, :], ACT.Tanh, scale=0.5), f"th{m}")
                    for m, name in ((1, "k"), (0, "q")):
                        dve(f"silu{m}")
                        done(fn(tmp[m][:, :], dc[:, m, :], ACT.Square), f"sq_{name}")
                    pe_("sum_k")
                    done(fn(tmp[1][:, :], B7, ACT.Sqrt, bias=eps_l2[:, :]), "std_k")
                    pe_("sum_q")
                    done(fn(tmp[0][:, :], B6, ACT.Sqrt, bias=eps_l2[:, :]), "std_q")
                    pe_("decay_rows")
                    done(fn(eg[:, :], B5, ACT.Exp), "exp_g")
                    drain(l, filled_before(h, "k_turned"))
                    dve("decay_min")
                    done(fn(dt_[:, :, :], dt_[:, :, :], ACT.Exp), "decay_exp")
                    dve("kd_arg")
                    done(fn(hc[:, 1, :], hc[:, 1, :], ACT.Exp), "kd_exp")
                    done(fn(hc[:, 0, :], hc[:, 0, :], ACT.Exp), "last_exp")
                    pe_("k_turned")
                    for c in range(CH):
                        last = fn(kg[:, c, :], tiles(B4)[:, c, :], ACT.Identity, scale=cols[:, 2, c, h:h + 1],
                                  bias=eps_0[:, :])
                    done(last, "kg")
                    pe_("v_turned")
                    done(fn(vk[:, :, :], tiles(B6), ACT.Copy, scale=0.5), "vk")
                    pe_("inv0_turned")
                    done(fn(tmp[0][:, :], B4, ACT.Copy), "inv0")
                    for s in range(1, LEVELS):
                        pe_(f"p{s}")
                        done(fn(tmp[2][:, :], B4, ACT.Copy), f"p{s}")
                    pe_("w")
                    done(fn(tmp[2][:, :], B4, ACT.Copy, scale=-1.0), "w")
                    pe_(f"o{CH - 1}")
                    done(fn(os_[:, :], B5, ACT.Copy, scale=0.5), "o")
                    done(fn(tmp[3][:, :], B5, ACT.Square), "o_sq")
                    pe_("rms_sums")
                    done(fn(tmp[1][:, :], B4, ACT.Sqrt, scale=1.0 / P, bias=eps_rms[:, :]), "rms_std")
                    done(fn(tmp[2][:, :], dz[:, h % 2, :], ACT.Tanh, scale=0.5), "z_th")
                    dve("y")
                    done(fn(yah[:, h, :], tmp[2][:, :], ACT.Copy), "y_hi")

            def merge(l):
                def split(d):
                    act.wait_ge(merged.sem, merged.at(l, d + 1))
                    fn(mh[:, d, :], xf[:, d, :], ACT.Copy).then_inc(merged_hi.sem, 1)

                for d in range(0, KD, 2):
                    drain(l, PARTS_TO[INDEX["gate", 0, d + 1]])
                    if d:
                        split(d - 2)
                        split(d - 1)
                split(KD - 2)
                split(KD - 1)

            def memory_kv(l):
                act.wait_ge(mem_loaded, l * 16 + 16)
                fn(meh[:, :, :], mraw[:, :, :], ACT.Copy).then_inc(mem_hi.sem, 1)

            def memory_kv_out(l):
                for n in range(KD):
                    tile_ready(l, "mem_k", n)
                    fn(xk[:, n, :], acc[:, n % 4, 0:MEM], ACT.Copy).then_inc(freed_a.sem, 1)
                for t in range(4):
                    tile_ready(l, "mem_v", t)
                    fn(xv[:, t // 2, (t % 2) * SEQ:(t % 2 + 1) * SEQ], acc[:, t, :], ACT.Copy).then_inc(freed_a.sem, 1)

            def cross_attention(l):
                with act.Fori(0, 2) as i:
                    for n in range(4):
                        tile_ready(l, "x_q", i * 4 + n)
                        fn(xq[:, i * 4 + n, :], acc[:, n, :], ACT.Copy, scale=(DM // HX) ** -0.5).then_inc(freed_a.sem, 1)

                def turned_copy(n):
                    h, i = divmod(n, CH)
                    act.wait_ge(x_turned.sem, x_turned.at(l, n + 1))
                    act.wait_ge(x_att_out.sem, x_att_out.at(l, 2 * h))
                    for j in range(KM):
                        last = fn(tmp[2 + j][:, i * P:(i + 1) * P], aux[:, 2 + n % 2, j * P:(j + 1) * P], ACT.Copy)
                    last.then_inc(x_turned_out.sem, 1)

                def out_copy(h):
                    for m in range(2):
                        act.wait_ge(x_att_out.sem, x_att_out.at(l, 2 * h + m + 1))
                        fn(oh[:, 2 * h + m, :], acc[:, 2 + m, :], ACT.Copy).then_inc(xo_hi.sem, 1)

                for n in range(HX * CH):
                    act.wait_ge(x_row_max.sem, x_row_max.at(l, n + 1))
                    if n >= 4:
                        act.wait_ge(x_turned.sem, x_turned.at(l, n - 3))
                    fn(x_sc(n), aux[:, n % 2, 0:MEM], ACT.Exp, bias=x_negmax[:, n:n + 1],
                       accum_out=x_sum[:, n:n + 1]).then_inc(x_exps.sem, 1)
                    if n >= 1:
                        turned_copy(n - 1)
                    if n >= 2 and (n - 1) % CH == 0:
                        out_copy((n - 1) // CH - 1)
                turned_copy(HX * CH - 1)
                out_copy(HX - 1)

            act.sem_inc(freed_a.sem, 4)
            act.wait_ge(x_loaded, 16)
            for k in range(KD):
                fn(xh[:, k, :], xf[:, k, :], ACT.Copy).then_inc(x_hi.sem, 1)
            with act.Fori(0, DEPTH) as l:
                act.wait_ge(x_hi.sem, x_hi.at(l, 0))
                act.dma_start(par[:, :], par_d[l]).then_inc(par_loaded, 16)
                ffn_inner(l, 0)
                out_projection(l, "ffn_down0", 0)
                act.wait_ge(sums_ready.sem, sums_ready.at(l, 1))
                act.dma_start(ba_w, ba_w_d[l]).then_inc(mix_par_loaded[1], 16)
                act.dma_start(ext[:, P - 1:3 * P - 1], table_d[l][:, 0:2 * P]).then_inc(mix_par_loaded[2], 16)
                layer_norm(l, 0)
                act.wait_ge(ext_padded.sem, ext_padded.at(l, 1))
                act.dma_start(ext_d, ext[:, :]).then_inc(ext_stored, 16)
                act.wait_ge(ext_stored, l * 16 + 16)
                act.dma_start(bias[:, :, :], bass.AP(tensor=ext_d.tensor, offset=0,
                                                     ap=[[1, P], [3 * P - 1, HA], [1, 2 * P]])).then_inc(bias_loaded, 16)
                attention(l)
                rg_lru(l)
                delta(l)
                merge(l)
                out_projection(l, "mix_out", 1)
                act.wait_ge(sums_ready.sem, sums_ready.at(l, 2))
                act.dma_start(mraw[:, :, :], memT.rearrange("(k p) t -> p k t", p=P)).then_inc(mem_loaded, 16)
                memory_kv(l)
                layer_norm(l, 1)
                memory_kv_out(l)
                cross_attention(l)
                out_projection(l, "x_out", 2)
                layer_norm(l, 2)
                ffn_inner(l, 1)
                out_projection(l, "ffn_down1", 3)
                layer_norm(l, 3)

        @block.vector
        def _(dve):
            chain = Chain(dve, dve_step)
            link = chain.link
            tt_, ts_, stt_ = dve.tensor_tensor, dve.tensor_scalar, dve.scalar_tensor_tensor

            def tile_ready(l, name, n):
                dve.wait_ge(acc_ready.sem, acc_ready.at(l, TILE0[name] + 1) + n)

            def low(dst, whole, high):
                return tt_(dst, whole, high.bitcast(F32), ALU.subtract)

            def ffn_inner(l, which):
                up = f"ffn_up{which}"
                with dve.Fori(0, KF // 2) as i:
                    for m in range(2):
                        j = i * 2 + m
                        dve.wait_ge(silu_th.sem, silu_th.at(l, which * KF + 1) + j)
                        stt_(tmp[1][:, :], tmp[0][:, :], 1.0, acc[:, 2 * m, :], ALU.add, ALU.mult).then_inc(freed_d.sem, 1)
                        dve.wait_ge(freed_d.sem, freed_d.at(l, FREE_D[up] + 2 * m + 1) + i * 4)
                        tile_ready(l, up, i * 4 + (2 * m + 1))
                        tt_(tmp[2][:, :], tmp[1][:, :], acc[:, 2 * m + 1, :], ALU.mult).then_inc(freed_d.sem, 1)
                        dve.wait_ge(inner_hi.sem, inner_hi.at(l, which * KF + 1) + j)
                        low(hl[:, j, :], tmp[2][:, :], hh[:, j, :]).then_inc(inner_lo.sem, 1)

            def out_projection(l, name, norm, factor, parts=False):
                link(dve.memset(y_sum[:, :], 0.0))
                link(dve.memset(sq_sum[:, :], 0.0))
                dve.sem_inc(waited_apart, 1)
                with dve.Fori(0, KD // 4) as i:
                    for n in range(4):
                        d = i * 4 + n
                        if parts:
                            tt_(xf[:, d, :], xh[:, d, :].bitcast(F32), xl[:, d, :].bitcast(F32), ALU.add).then_inc(x_whole.sem, 1)
                            dve.wait_ge(x_whole.sem, x_whole.at(l, 1) + d)
                        tile_ready(l, name, d)
                        stt_(xf[:, d, :], acc[:, n, :], factor, xf[:, d, :], ALU.mult, ALU.add).then_inc(freed_d.sem, 1)
                        dve.wait_ge(freed_d.sem, freed_d.at(l, FREE_D[name] + 1) + d)
                        wait_apart(dve, y_added.sem, y_added.at(l, norm * KD) + d)
                        tt_(y_sum[:, :], y_sum[:, :], xf[:, d, :], ALU.add).then_inc(y_added.sem, 1)
                        dve.wait_ge(y_sq.sem, y_sq.at(l, norm * KD + 1) + d)
                        wait_apart(dve, sq_added.sem, sq_added.at(l, norm * KD) + d)
                        tt_(sq_sum[:, :], sq_sum[:, :], tmp[3][:, :], ALU.add).then_inc(sq_added.sem, 1)

            def layer_norm(l, norm):
                dve.wait_ge(sums_ready.sem, sums_ready.at(l, norm + 1))
                link(dve.tensor_copy(tmp[1][:, :], B4))
                link(tt_(tmp[2][:, :], tmp[1][:, :], tmp[1][:, :], ALU.mult))
                link(stt_(tmp[3][:, :], tmp[2][:, :], -1.0, B5, ALU.mult, ALU.add))
                ts_(tmp[3][:, :], tmp[3][:, :], 0.0, LN_EPS / ALPHA ** 2, ALU.max, ALU.add).then_inc(variance.sem, 1)
                dve.wait_ge(deviation.sem, deviation.at(l, norm + 1))
                link(dve.reciprocal(tmp[0][:, :], tmp[0][:, :]))
                link(tt_(tmp[1][:, :], tmp[1][:, :], tmp[0][:, :], ALU.mult))

                def split(d):
                    dve.wait_ge(x_hi.sem, x_hi.at(l, norm * KD + d + 1))
                    low(xl[:, d, :], xf[:, d, :], xh[:, d, :]).then_inc(x_lo.sem, 1)

                for d in range(KD):
                    link(tt_(xf[:, d, :], xf[:, d, :], tmp[0][:, :], ALU.mult))
                    tt_(xf[:, d, :], xf[:, d, :], tmp[1][:, :], ALU.subtract).then_inc(centred.sem, 1)
                    if d >= 1:
                        split(d - 1)
                split(KD - 1)

            def softplus(out, x, e, t, u, n_rows):
                link(ts_(t, e, 2.0, None, ALU.add))
                link(dve.reciprocal(t, t))
                link(tt_(t, e, t, ALU.mult))
                link(tt_(u, t, t, ALU.mult))
                link(ts_(e, u, 1.0 / 15, None, ALU.mult))
                for k in range(6, 0, -1):
                    link(stt_(e, e, 1.0 / (2 * k + 1), u, ALU.add, ALU.mult))
                link(stt_(e, e, 1.0, t, ALU.add, ALU.mult))
                link(ts_(out, x, 0.0, None, ALU.max))
                return stt_(out, e, 2.0, out, ALU.mult, ALU.add)

            def attention(l):
                dve.wait_ge(mix_par_loaded[2], l * 16 + 16)
                dve.tensor_copy(ext[:, 0:P - 1], ext[:, P - 1:P].broadcast_to([HA, P - 1])).then_inc(ext_padded.sem, 1)
                lru_rates(l)
                delta_rows(l)
                lru_rates_out(l)
                for m in range(4):
                    dve.wait_ge(bias_flipped.sem, bias_flipped.at(l, 4))
                    dve.tensor_copy(bias[:, 2 * m:2 * m + 2, :], aux[:, m, :].rearrange("p (h k) -> p h k", h=2)).then_inc(bias_copied.sem, 1)
                dve.wait_ge(bias_copied.sem, bias_copied.at(l, 4))
                dve.memset(bias[0:P // 2, :, 3 * P // 2:2 * P], NEG).then_inc(bias_masked.sem, 1)
                dve.wait_ge(bias_masked.sem, bias_masked.at(l, 1))

                def normalise(n):
                    s = sc[:, n % CH, 0:(n % CH + 1) * P]
                    dve.wait_ge(exps.sem, exps.at(l, n + 1))
                    link(dve.reciprocal(inv_sum[:, n:n + 1], row_sum[:, n:n + 1]))
                    ts_(s, s, inv_sum[:, n:n + 1], None, ALU.mult).then_inc(probs.sem, 1)

                def out_low(pair):
                    dve.wait_ge(yc_hi.sem, yc_hi.at(l, pair + 1))
                    low(ycl[:, KB + pair, :], acc[:, pair % 2, :], ych[:, KB + pair, :]).then_inc(yc_lo.sem, 1)

                for n in range(HA * CH):
                    h, i = divmod(n, CH)
                    bank = aux[:, n % 2, :]
                    if n >= CH:
                        dve.wait_ge(turned.sem, turned.at(l, n - CH + 1))
                    dve.wait_ge(scores.sem, scores.at(l, n + 1))
                    if i >= 2:
                        far = slice(0, (i - 1) * P)
                        ts_(sc[:, i, far], bank[:, far], bias[:, h, 0:1], None, ALU.add)
                    near = slice(max(i - 1, 0) * P, (i + 1) * P)
                    tt_(sc[:, i, near], bank[:, near], bias[:, h, (0 if i else P):2 * P], ALU.add).then_inc(biased.sem, 1)
                    dve.wait_ge(biased.sem, biased.at(l, n + 1))
                    dve.tensor_reduce(neg_max[:, n:n + 1], sc[:, i, 0:(i + 1) * P], AX.X, ALU.max, negate=True).then_inc(row_max.sem, 1)
                    if n >= 1:
                        normalise(n - 1)
                    if n >= 2 and (n - 1) % (2 * CH) == 0:
                        out_low((n - 1) // (2 * CH) - 1)
                    lru_beside(l, n)
                normalise(HA * CH - 1)
                out_low(KB - 1)
                for n in range(HA * CH, LRU_BESIDE_END):
                    lru_beside(l, n)

            def col(c):
                return par[:, c:c + 1]

            def conv_part(n, dst, src, weight, add=None):
                if n == 0:
                    if add is None:
                        return ts_(dst, src, weight(3), None, ALU.mult)
                    return ts_(dst, src, weight(3), add, ALU.mult, ALU.add)
                return stt_(dst[:, n:], src[:, 0:SEQ - n], weight(3 - n), dst[:, n:], ALU.mult, ALU.add)

            def conv(*args):
                for n in range(3):
                    link(conv_part(n, *args))
                return conv_part(3, *args)

            def lru_rates(l):
                lam_p = par[:, P_LAM:P_LAM + KB]
                link(ts_(lam[:, 0, :], lam_p, -1.0, None, ALU.mult))
                tt_(lam[:, 1, :], lam[:, 0, :], lam_p, ALU.max).then_inc(lam_arg.sem, 1)
                link(ts_(lam[:, 6:8, :], par[:, P_GB:P_GB + 2 * KB].rearrange("p (g k) -> p g k", g=2), 0.5, None, ALU.mult))

            def lru_rates_out(l):
                dve.wait_ge(lam_exp.sem, lam_exp.at(l, 1))
                link(softplus(lam[:, 5, :], lam[:, 0, :], lam[:, 2, :], lam[:, 3, :], lam[:, 4, :], P))
                link(ts_(lam[:, 4, :], lam[:, 5, :], -LRU_C / 2, None, ALU.mult))
                ts_(lam[:, 5, :], lam[:, 5, :], LRU_C / 2, None, ALU.mult).then_inc(lam_ready.sem, 1)

            def lru_beside(l, n):
                step, p, part = LRU_BESIDE_DVE.get(n, (None, None, None))
                if step == "conv":
                    dve.wait_ge(freed_a.sem, freed_a.at(l, FREE_A["lru_x"] + p + 1))
                    ins = conv_part(part, lc[:, p, :], lx[:, p, :], lambda tap: col(P_LCW + 4 * p + tap), col(P_LCB + p))
                    link(ins) if part < 3 else lru_dve.done(ins, f"conv{p}")
                elif step == "g_arg":
                    if part == 0:
                        dve.wait_ge(lru_act.sem, lru_act.after(l, 0, f"g_sq{p}"))
                        link(ts_(tmp[0][:, :], tmp[0][:, :], 0.044715, 1.0, ALU.mult, ALU.add))
                    else:
                        dve.wait_ge(freed_a.sem, freed_a.at(l, FREE_A["lru_g"] + p + 1))
                        lru_dve.done(tt_(tmp[0][:, :], tmp[0][:, :], lg[:, p, :], ALU.mult), f"g_arg{p}")
                elif step == "g_gate":
                    dve.wait_ge(lru_act.sem, lru_act.after(l, 0, f"g_th{p}"))
                    lru_dve.done(stt_(lg[:, p, :], tmp[1][:, :], 1.0, lg[:, p, :], ALU.add, ALU.mult), f"g_gate{p}")

            def rg_lru(l):
                def act_(step):
                    dve.wait_ge(lru_act.sem, lru_act.after(l, 0, step))
                done = lru_dve.done

                def own(step):
                    dve.wait_ge(lru_dve.sem, lru_dve.after(l, 0, step))

                def low_part(p):
                    act_(f"y_hi{p}")
                    done(low(ycl[:, p, :], tmp[p % 2][:, :], ych[:, p, :]), f"y_lo{p}")

                for p in range(KB):
                    act_(f"s{p}")
                    if p:
                        own(f"q{p - 1}")
                    link(ts_(tmp[0][:, :], lr[:, p, :], 1.0, None, ALU.add))
                    link(dve.reciprocal(tmp[0][:, :], tmp[0][:, :]))
                    done(tt_(lr[:, p, :], lr[:, p, :], tmp[0][:, :], ALU.mult), f"q{p}")
                    done(stt_(li[:, p, :], li[:, p, :], 1.0, lc[:, p, :], ALU.add, ALU.mult), f"xi{p}")
                for p in range(KB):
                    act_(f"q{p}")
                    link(tt_(li[:, p, :], li[:, p, :], lr[:, p, :], ALU.mult))
                    done(dve.tensor_tensor_scan(lc[:, p, :], lx[:, p, :], li[:, p, :], 0.0, ALU.mult, ALU.add), f"h{p}")
                    own(f"h{p}")
                    if p >= 2:
                        own(f"y_lo{p - 2}")
                    done(stt_(tmp[p % 2][:, :], lc[:, p, :], 0.5, lg[:, p, :], ALU.mult, ALU.mult), f"y{p}")
                    if p:
                        low_part(p - 1)
                low_part(KB - 1)

            def delta_rows(l):
                link(dve.memset(rows[:, :], 0.0))
                r = slice(0, HN)
                dve.wait_ge(ba_ready.sem, ba_ready.at(l, 1))
                link(ts_(row_f, B7[r, :], par[r, P_DT:P_DT + 1], None, ALU.add))
                link(ts_(tmp[0][r, :], row_f, -1.0, None, ALU.mult))
                tt_(tmp[0][r, :], tmp[0][r, :], row_f, ALU.max).then_inc(row_arg.sem, 1)
                dve.wait_ge(row_exp.sem, row_exp.at(l, 1))
                link(softplus(row_f, row_f, tmp[1][r, :], tmp[2][r, :], tmp[3][r, :], HN))
                link(ts_(nea[r, 1:2], nea[r, 0:1], -1.0, None, ALU.mult))
                link(ts_(row_f, row_f, nea[r, 1:2], None, ALU.mult))
                for c in range(CH):
                    tok = slice(c * P, (c + 1) * P)
                    link(dve.tensor_tensor_scan(rows[r, tok], ones[r, :], row_f[:, tok], 0.0, ALU.mult, ALU.add))
                dve.wait_ge(beta_th.sem, beta_th.at(l, 1))
                b = slice(32, 32 + HN)
                ts_(rows[b, :], rows[b, :], 0.5, 0.5, ALU.mult, ALU.add).then_inc(rows_ready.sem, 1)
                dve.wait_ge(rows_turned.sem, rows_turned.at(l, 1))
                link(dve.tensor_copy(cols[:, 1, :, :], tiles(B6)[:, :, 32:32 + HN]))
                dve.tensor_copy(cols[:, 0, :, :], tiles(B6)[:, :, 0:HN]).then_inc(cols_ready.sem, 1)

            drained = [KB]

            def mixer_tile(l, t):
                r, d = MIXER[t][1:3]
                g = INDEX["gate", r, d]
                dve.wait_ge(freed_a.sem, freed_a.at(l, FREE_A["mixer"] + MIXER_A[g]))
                tile_ready(l, "mixer", t)
                gate = gt[:, r - 1 if r else d % 2, :]
                freed = freed_d.at(l, FREE_D["mixer"] + MIXER_D[t])
                if r == 1:
                    stt_(xf[:, d, :], gate, 1.0, acc[:, t % 4, :], ALU.add, ALU.mult).then_inc(freed_d.sem, 1)
                    return
                stt_(gate, gate, 1.0, acc[:, t % 4, :], ALU.add, ALU.mult).then_inc(freed_d.sem, 1)
                dve.wait_ge(freed_d.sem, freed)
                if r == 0:
                    dve.wait_ge(partial.sem, partial.at(l, d + 1))
                tt_(xf[:, d, :], xf[:, d, :], gate, ALU.add).then_inc((partial if r else merged).sem, 1)

            def drain(l, count):
                while drained[0] < len(MIXER) and PARTS_TO[drained[0]] <= count:
                    if MIXER[drained[0]][0] == "up":
                        mixer_tile(l, drained[0])
                    drained[0] += 1

            def delta(l):
                for h in range(HN):
                    def act_(step):
                        dve.wait_ge(dn_act.sem, dn_act.after(l, h, step))

                    def pe_(step):
                        drain(l, filled_before(h, step))
                        dve.wait_ge(dn_pe.sem, dn_pe.after(l, h, step))

                    def own(step):
                        dve.wait_ge(dn_dve.sem, dn_dve.after(l, h, step))
                    done = dn_dve.done

                    def wide(x):
                        return x.rearrange("p (a b) -> p a b", a=1).broadcast_to([P, CH, P])
                    for m in (1, 0, 2):
                        dve.wait_ge(freed_a.sem, freed_a.at(l, FREE_A["mixer"] + MIXER_A[INDEX["proj", h, m]]))
                        done(conv(dc[:, m, :], dx[:, m, :], lambda tap: col(12 * h + P_CW + 4 * m + tap)), f"conv{m}")
                    for m in (1, 0, 2):
                        act_(f"th{m}")
                        done(stt_(dc[:, m, :], tmp[m][:, :], 1.0, dc[:, m, :], ALU.add, ALU.mult), f"silu{m}")
                    done(ts_(mt[0:HN, :, :].rearrange("p c m -> p (c m)"), rows[0:HN, :], const[0:HN, h:h + 1], None, ALU.mult), "g_row")
                    drain(l, filled_before(h, "sum_k"))
                    act_("std_k")
                    link(dve.reciprocal(tmp[1][:, :], tmp[1][:, :]))
                    done(tt_(dc[:, 1, :], dc[:, 1, :], tmp[1][:, :], ALU.mult), "k_normed")
                    act_("std_q")
                    link(dve.reciprocal(tmp[0][:, :], tmp[0][:, :]))
                    done(stt_(dc[:, 0, :], dc[:, 0, :], float(P) ** -0.5, tmp[0][:, :], ALU.mult, ALU.mult), "q_normed")
                    act_("exp_g")
                    done(dve.tensor_copy(hc[:, 0, :].rearrange("p (c a) -> p c a", a=1), tiles(B5)[:, :, P - 1:P]), "g_last")
                    for c in range(CH):
                        last = ts_(dt_[:, c, :], tiles(B5)[:, c, :], cols[:, 0, c, h:h + 1], 0.0, ALU.subtract, ALU.min)
                    done(last, "decay_min")
                    own("g_last")
                    done(tt_(hc[:, 1, :].rearrange("p (c a) -> p c a", a=1), hc[:, 0, :].rearrange("p (c a) -> p c a", a=1),
                             cols[:, 0, :, h:h + 1], ALU.subtract), "kd_arg")
                    act_("decay_exp")
                    done(tt_(dt_[:, :, :], dt_[:, :, :], wide(causal), ALU.mult), "decay")
                    act_("kg")
                    for c in range(CH):
                        last = ts_(kd[:, c, :], tiles(B4)[:, c, :], hc[:, 1, c:c + 1], None, ALU.mult)
                    done(last, "kd")
                    own("decay")
                    pe_("a01")
                    pe_("a23")
                    for part in range(2):
                        for c in range(CH):
                            o = tiles((B7, B5)[c // 2])[:, 2 * (c % 2) + part, :]
                            if part == 0:
                                last = stt_(mt[:, c, :], o, cols[:, 1, c, h:h + 1], dt_[:, c, :], ALU.mult, ALU.mult)
                            else:
                                last = tt_(qk[:, c, :], o, dt_[:, c, :], ALU.mult)
                        done(last, ("m", "qk")[part])
                    own("m")
                    done(tt_(tiles(tmp[1]), mt[:, :, :], level_mask(0), ALU.mult), "c0")
                    own("c0")
                    own("qk")
                    done(tt_(tt[:, :, :], wide(ident), tiles(tmp[1]), ALU.subtract), "t0")
                    done(tt_(dc[:, 0, :], dc[:, 0, :], eg[:, :], ALU.mult), "q_dec")
                    for s in range(1, LEVELS):
                        if s == 1:
                            own("t0")
                        done(tt_(tiles(tmp[1]), mt[:, :, :], level_mask(s), ALU.mult), f"c{s}")
                        pe_(f"q{s}" if s < LEVELS - 1 else f"qt{s}")
                        done(tt_(tt[:, :, :], tt[:, :, :], tiles(B6), ALU.subtract), f"t{s}")
                        if s < LEVELS - 1:
                            done(tt_(tmp[0][:, :], tmp[0][:, :], B7, ALU.subtract), f"n{s}")
                    for c in range(CH):
                        pe_(f"v{c}")
                        done(ts_(vn[:, :], B6[:, 0:P], cols[:, 1, c, h:h + 1], None, ALU.mult), f"v{c}")
                        if c < CH - 1:
                            pe_(f"s{c}")
                            if c == 0:
                                done(dve.tensor_copy(state[:, :], B7[:, 0:P]), "s0")
                            else:
                                act_("last_exp")
                                done(stt_(state[:, :], state[:, :], hc[:, 0, c:c + 1], B7[:, 0:P], ALU.mult, ALU.add), f"s{c}")
                    drain(l, filled_before(h, "rms_sums"))
                    act_("rms_std")
                    link(dve.reciprocal(tmp[1][:, :], tmp[1][:, :]))
                    done(tt_(os_[:, :], os_[:, :], tmp[1][:, :], ALU.mult), "o_normed")
                    act_("z_th")
                    done(stt_(tmp[2][:, :], tmp[2][:, :], 1.0, dz[:, h % 2, :], ALU.add, ALU.mult), "z_gate")
                    own("z_gate")
                    done(stt_(tmp[2][:, :], tmp[2][:, :], par[:, P_NW:P_NW + 1], os_[:, :], ALU.mult, ALU.mult), "y")
                    act_("y_hi")
                    done(low(yal[:, h, :], tmp[2][:, :], yah[:, h, :]), "y_lo")

            def merge(l):
                def low_part(d):
                    dve.wait_ge(merged_hi.sem, merged_hi.at(l, d + 1))
                    low(ml[:, d, :], xf[:, d, :], mh[:, d, :]).then_inc(merged_lo.sem, 1)

                for d in range(0, KD, 2):
                    drain(l, PARTS_TO[INDEX["up", 0, d + 1]])
                    if d:
                        low_part(d - 2)
                        low_part(d - 1)
                low_part(KD - 2)
                low_part(KD - 1)
                dve.wait_ge(merged_lo.sem, merged_lo.at(l, KD))

            def cross_attention(l):
                def normalise(n):
                    dve.wait_ge(x_exps.sem, x_exps.at(l, n + 1))
                    link(dve.reciprocal(x_inv[:, n:n + 1], x_sum[:, n:n + 1]))
                    ts_(x_sc(n), x_sc(n), x_inv[:, n:n + 1], None, ALU.mult).then_inc(x_probs.sem, 1)

                def out_low(h):
                    for m in range(2):
                        dve.wait_ge(xo_hi.sem, xo_hi.at(l, 2 * h + m + 1))
                        low(ol[:, 2 * h + m, :], acc[:, 2 + m, :], oh[:, 2 * h + m, :]).then_inc(xo_lo.sem, 1)

                for n in range(HX * CH):
                    dve.wait_ge(x_scores.sem, x_scores.at(l, n + 1))
                    dve.tensor_reduce(x_negmax[:, n:n + 1], aux[:, n % 2, 0:MEM], AX.X, ALU.max, negate=True).then_inc(x_row_max.sem, 1)
                    if n >= 1:
                        normalise(n - 1)
                    if n >= 2 and (n - 1) % CH == 0:
                        out_low((n - 1) // CH - 1)
                normalise(HX * CH - 1)
                out_low(HX - 1)

            dve.sem_inc(freed_d.sem, 4)
            dve.sem_inc(y_added.sem, 1)
            dve.sem_inc(sq_added.sem, 1)
            dve.wait_ge(consts_set, 5)
            dve.wait_ge(const_loaded, 16)
            for k in range(KD):
                dve.wait_ge(x_hi.sem, k + 1)
                low(xl[:, k, :], xf[:, k, :], xh[:, k, :]).then_inc(x_lo.sem, 1)
            with chain.loop(DEPTH, LAYER_LINKS) as l:
                ffn_inner(l, 0)
                out_projection(l, "ffn_down0", 0, HALF_STEP)
                layer_norm(l, 0)
                dve.wait_ge(par_loaded, l * 16 + 16)
                attention(l)
                rg_lru(l)
                delta(l)
                merge(l)
                out_projection(l, "mix_out", 1, GATE_STEP, parts=True)
                dve.wait_ge(mem_hi.sem, mem_hi.at(l, 1))
                low(mel[:, :, :], mraw[:, :, :], meh[:, :, :]).then_inc(mem_lo.sem, 1)
                layer_norm(l, 1)
                cross_attention(l)
                out_projection(l, "x_out", 2, 1.0 / ALPHA)
                layer_norm(l, 2)
                ffn_inner(l, 1)
                out_projection(l, "ffn_down1", 3, HALF_STEP)
                layer_norm(l, 3)


def pack(x, mem, ln_g, ln_b, ffn_w12, ffn_w3, mix_w_in, dn_conv_w, dn_a_log, dn_dt_bias, dn_norm_w, lru_conv_w,
         lru_conv_b, lru_gate_w, lru_gate_b, lru_lambda, la_rel_bias, w_branch, mix_w_out, xa_wq, xa_wkv, xa_wo):
    A = np.asarray

    def stationary(w):
        k, m = w.shape
        return w.reshape(k // P, P, m // P, P).transpose(2, 1, 0, 3).reshape(m // P, P, -1)

    def padded(u, columns):
        out = np.zeros(u.shape[:-1] + (columns,), u.dtype)
        out[..., :u.shape[-1]] = u
        return out

    def units(w):
        n = -(-w.shape[-1] // UNIT)
        return padded(w, n * UNIT).reshape(len(w), P, n, UNIT).transpose(0, 2, 1, 3).reshape(-1, P, UNIT)

    def moving(w):
        k, m = w.shape
        per = UNIT // m
        return w.reshape(k // P // per, per, P, m).transpose(0, 2, 1, 3).reshape(-1, P, UNIT)

    q, kk, v, z, bb, aa, lx_, lg_, aq_, ak_, av_, gl = np.split(
        np.arange(mix_w_in.shape[2]), np.cumsum([BRW] * 4 + [HN] * 2 + [BRW] * 5))
    stream, par, ba, gw = [], [], [], []
    for l in range(DEPTH):
        w_in = A(mix_w_in[l])

        def cols_of(idx):
            return stationary(w_in[:, idx])

        def ffn(n):
            up = stationary(A(ffn_w12[l, n]))
            return [up.reshape(2, KF, P, UNIT).transpose(1, 0, 2, 3).reshape(-1, P, UNIT),
                    units(stationary(A(ffn_w3[l, n])))]
        stream += ffn(0)
        stream += [cols_of(aq_), cols_of(ak_), moving(w_in[:, av_]), cols_of(lx_), cols_of(lg_)]
        proj = np.stack([cols_of(i) for i in (q, kk, v, z)], 1)
        gates = cols_of(gl).reshape(NBR, KD, P, UNIT)
        branch = stationary(A(w_branch[l]).reshape(NBR * BRW, DM)).reshape(KD, P, NBR, BRW).transpose(2, 0, 1, 3)
        for kind, a, b, _, at in MIXER:
            if kind == "proj":
                stream.append(proj[a, b][None])
            elif kind == "gate":
                stream.append(gates[a, b][None])
            elif at == 0:
                stream.append(np.concatenate([branch[1, b], branch[2, b]] if a else [branch[0, b], branch[0, b + 1]], 1)[None])
        stream += [stationary(A(mix_w_out[l])), stationary(A(xa_wkv[l])[:, :DM]), moving(A(xa_wkv[l])[:, DM:]),
                   stationary(A(xa_wq[l])), stationary(A(xa_wo[l]))]
        stream += ffn(1)

        def by_tile(a, n):
            return A(a).reshape(n, P).T
        cw = A(dn_conv_w[l]).reshape(4, 3, HN, P).transpose(3, 2, 1, 0).reshape(P, -1)
        lcw = A(lru_conv_w[l]).reshape(4, KB, P).transpose(2, 1, 0).reshape(P, -1)

        def rows(a):
            out = np.zeros((P, 1), np.float32)
            out[:HN, 0] = A(a)
            return out
        par.append(np.concatenate([
            by_tile(ln_g[l], 4 * KD), by_tile(ln_b[l], 4 * KD), cw, lcw, by_tile(lru_conv_b[l], KB),
            by_tile(lru_gate_b[l], 2 * KB), by_tile(lru_lambda[l], KB), A(dn_norm_w[l])[:, None],
            rows(dn_a_log[l]), rows(dn_dt_bias[l])], 1))
        b = np.zeros((P, KD, 64), np.float32)
        b[:, :, 0:HN] = w_in[:, aa].reshape(KD, P, HN).transpose(1, 0, 2)
        b[:, :, 32:32 + HN] = w_in[:, bb].reshape(KD, P, HN).transpose(1, 0, 2)
        ba.append(b)
        g = np.zeros((P, 2, KB, P), np.float32)
        for n in range(2 * KB):
            half = slice(64 * (n % 2), 64 * (n % 2) + 64)
            g[half, :, n // 2, half] = A(lru_gate_w[l])[:, n].transpose(1, 0, 2)
        gw.append(g)
    i = np.arange(P)
    const = [np.eye(P), i[:, None] <= i[None, :], np.eye(P)[::-1]]
    for s in range(LEVELS):
        b = 1 << s
        const.append((i[:, None] // b % 2 == 0) & (i[None, :] // b == i[:, None] // b + 1))
    return {"in_xT": np.ascontiguousarray(A(x)[0].T), "in_memT": np.ascontiguousarray(A(mem)[0].T),
            "in_stream": np.concatenate(stream, 0), "in_par": np.stack(par), "in_ba_w": np.stack(ba),
            "in_gate_w": np.stack(gw), "in_table": A(la_rel_bias), "in_const": np.concatenate(const, 1).astype(np.float32)}


def kernel(**inputs):
    import concourse.bacc as bacc
    from concourse.bass_utils import run_bass_kernel_spmd

    nc = bacc.Bacc("TRN2", target_bir_lowering=False, num_devices=1)
    arrays = pack(**inputs)
    ins = {n: nc.dram_tensor(n, a.shape, mybir.dt.from_np(a.dtype), kind="ExternalInput").ap() for n, a in arrays.items()}
    ext_d = nc.dram_tensor("rel_scratch", (HA, 3 * P - 1), F32).ap()
    out = nc.dram_tensor("out_xT", (DM, SEQ), F32, kind="ExternalOutput").ap()
    trunk(nc, ins["in_xT"], ins["in_memT"], ins["in_stream"], ins["in_par"], ins["in_ba_w"], ins["in_gate_w"],
          ins["in_table"], ins["in_const"], ext_d, out)
    got = run_bass_kernel_spmd(nc, [arrays], core_ids=[0]).results[0]["out_xT"]
    return np.ascontiguousarray(got.T)[None]
```
